# Optimizing a Trainium2 kernel written in Bass

```python
import math
import jax, jax.numpy as jnp
from jax import lax
import numpy as np
import jax
import jax.numpy as jnp

D_MODEL = 1024
BATCH = 1
SEQ = 256
DEPTH = 2

N_MIXERS = 2
N_A = (DEPTH + 1) // 2
N_B = DEPTH // 2

LRU_WIDTH = D_MODEL
N_LRU_BLOCKS = 4
LRU_BLOCK = LRU_WIDTH // N_LRU_BLOCKS
CONV_WIDTH = 4
LRU_C = 8.0
A_MIN = 0.9
A_MAX = 0.999

HEAD_DIM = 64
N_HEADS = D_MODEL // HEAD_DIM
Q_BLOCK = 128

D_FF = int(math.ceil(8 * D_MODEL / 3 / 256)) * 256

RMS_EPS = 1e-6


def rms_norm(x, g):
    xf = x.astype(jnp.float32)
    y = xf * lax.rsqrt(jnp.mean(xf * xf, axis=-1, keepdims=True) + RMS_EPS)
    return (y * g.astype(jnp.float32)).astype(x.dtype)

def causal_depthwise_conv(x, w, b):
    c = x.shape[-1]
    y = lax.conv_general_dilated(
        x, w.reshape(CONV_WIDTH, 1, c).astype(x.dtype),
        window_strides=(1,), padding=[(CONV_WIDTH - 1, 0)],
        dimension_numbers=("NWC", "WIO", "NWC"), feature_group_count=c)
    return y + b

def _linear_recurrence_combine(e1, e2):
    a1, b1 = e1
    a2, b2 = e2
    return a1 * a2, a2 * b1 + b2

def rg_lru_block(x, w_in, b_in, conv_w, conv_b, gate_w, gate_b, lam, w_out, b_out):
    bsz, seq, _ = x.shape
    u = jnp.einsum("bsd,de->bse", x, w_in) + b_in
    gate_branch, rec = u[..., :LRU_WIDTH], u[..., LRU_WIDTH:]
    rec = causal_depthwise_conv(rec, conv_w, conv_b)
    rec_blk = rec.reshape(bsz, seq, N_LRU_BLOCKS, LRU_BLOCK)
    gl = jnp.einsum("bsnc,gncd->gbsnd", rec_blk, gate_w).reshape(2, bsz, seq, LRU_WIDTH)
    gl = gl.astype(jnp.float32) + gate_b.astype(jnp.float32)[:, None, None, :]
    r_gate = jax.nn.sigmoid(gl[0])
    i_gate = jax.nn.sigmoid(gl[1])
    log_a = -LRU_C * r_gate * jax.nn.softplus(-lam.astype(jnp.float32))
    a = jnp.exp(log_a)
    mult = jnp.sqrt(-jnp.expm1(2.0 * log_a))
    b = mult * (i_gate * rec.astype(jnp.float32))
    _, h = lax.associative_scan(_linear_recurrence_combine, (a, b), axis=1)
    y = jax.nn.gelu(gate_branch, approximate=True) * h.astype(x.dtype)
    return jnp.einsum("bse,ed->bsd", y, w_out) + b_out

def stick_breaking_attention(x, w_qkv, w_o):
    bsz, seq, _ = x.shape
    qkv = jnp.einsum("bsd,de->bse", x, w_qkv).reshape(bsz, seq, 3, N_HEADS, HEAD_DIM)
    q = jnp.transpose(qkv[:, :, 0], (0, 2, 1, 3))
    k = jnp.transpose(qkv[:, :, 1], (0, 2, 1, 3))
    v = jnp.transpose(qkv[:, :, 2], (0, 2, 1, 3))
    scale = 1.0 / math.sqrt(HEAD_DIM)
    outs = []
    for blk in range(seq // Q_BLOCK):
        t0 = blk * Q_BLOCK
        t1 = t0 + Q_BLOCK
        qb = q[:, :, t0:t1]
        kb = k[:, :, :t1]
        vb = v[:, :, :t1]
        z = jnp.einsum("bhqd,bhkd->bhqk", qb, kb).astype(jnp.float32) * scale
        t_idx = t0 + jnp.arange(Q_BLOCK)[:, None]
        s_idx = jnp.arange(t1)[None, :]
        strict = s_idx < t_idx
        log_fail = jnp.where(strict, jax.nn.log_sigmoid(-z), 0.0)
        suffix = lax.cumsum(log_fail, axis=3, reverse=True) - log_fail
        weights = jnp.where(strict, jnp.exp(jax.nn.log_sigmoid(z) + suffix), 0.0)
        outs.append(jnp.einsum("bhqk,bhkd->bhqd", weights.astype(vb.dtype), vb))
    o = jnp.concatenate(outs, axis=2)
    o = jnp.transpose(o, (0, 2, 1, 3)).reshape(bsz, seq, N_HEADS * HEAD_DIM)
    return jnp.einsum("bse,ed->bsd", o, w_o)

def swiglu_ffn(x, w_in, w_out):
    gu = jnp.einsum("bsd,df->bsf", x, w_in)
    h = jax.nn.silu(gu[..., :D_FF]) * gu[..., D_FF:]
    return jnp.einsum("bsf,fd->bsd", h, w_out)

def first_inputs(seed: int = 0) -> dict:
    key = jax.random.key(seed)
    ks = jax.random.split(key, 20)
    f32 = jnp.float32

    def nrm(k, shape, fan_in):
        return jax.random.normal(k, shape, f32) * (fan_in ** -0.5)

    x = jax.random.normal(ks[0], (BATCH, SEQ, D_MODEL), f32)
    mix_norm = 1.0 + 0.05 * jax.random.normal(ks[1], (DEPTH, D_MODEL), f32)
    ffn_norm = 1.0 + 0.05 * jax.random.normal(ks[2], (DEPTH, D_MODEL), f32)
    final_norm = 1.0 + 0.05 * jax.random.normal(ks[3], (D_MODEL,), f32)

    lru_w_in = nrm(ks[4], (N_A, D_MODEL, 2 * LRU_WIDTH), D_MODEL)
    lru_b_in = 0.02 * jax.random.normal(ks[5], (N_A, 2 * LRU_WIDTH), f32)
    lru_conv_w = nrm(ks[6], (N_A, CONV_WIDTH, LRU_WIDTH), CONV_WIDTH)
    lru_conv_b = 0.02 * jax.random.normal(ks[7], (N_A, LRU_WIDTH), f32)
    lru_gate_w = nrm(ks[8], (N_A, 2, N_LRU_BLOCKS, LRU_BLOCK, LRU_BLOCK), LRU_BLOCK)
    lru_gate_b = 0.02 * jax.random.normal(ks[9], (N_A, 2, LRU_WIDTH), f32)
    u = jax.random.uniform(ks[10], (N_A, LRU_WIDTH), f32, A_MIN, A_MAX)
    a0 = u ** (1.0 / LRU_C)
    lru_lambda = jnp.log(a0) - jnp.log1p(-a0)
    lru_w_out = nrm(ks[11], (N_A, LRU_WIDTH, D_MODEL), LRU_WIDTH)
    lru_b_out = 0.02 * jax.random.normal(ks[12], (N_A, D_MODEL), f32)

    attn_w_qkv = nrm(ks[13], (N_B, D_MODEL, 3 * N_HEADS * HEAD_DIM), D_MODEL)
    attn_w_o = nrm(ks[14], (N_B, N_HEADS * HEAD_DIM, D_MODEL), N_HEADS * HEAD_DIM)

    ffn_w_in = nrm(ks[15], (DEPTH, D_MODEL, 2 * D_FF), D_MODEL)
    ffn_w_out = nrm(ks[16], (DEPTH, D_FF, D_MODEL), D_FF)

    return {
        "x": x, "mix_norm": mix_norm, "ffn_norm": ffn_norm, "final_norm": final_norm,
        "lru_w_in": lru_w_in, "lru_b_in": lru_b_in, "lru_conv_w": lru_conv_w,
        "lru_conv_b": lru_conv_b, "lru_gate_w": lru_gate_w, "lru_gate_b": lru_gate_b,
        "lru_lambda": lru_lambda, "lru_w_out": lru_w_out, "lru_b_out": lru_b_out,
        "attn_w_qkv": attn_w_qkv, "attn_w_o": attn_w_o,
        "ffn_w_in": ffn_w_in, "ffn_w_out": ffn_w_out,
    }

def first_block(x, mix_norm, ffn_norm, final_norm, lru_w_in, lru_b_in, lru_conv_w,
              lru_conv_b, lru_gate_w, lru_gate_b, lru_lambda, lru_w_out, lru_b_out,
              attn_w_qkv, attn_w_o, ffn_w_in, ffn_w_out):
    h = x
    for layer in range(DEPTH):
        mixer = layer % N_MIXERS
        j = layer // N_MIXERS
        hn = rms_norm(h, mix_norm[layer])
        if mixer == 0:
            mixed = rg_lru_block(hn, lru_w_in[j], lru_b_in[j], lru_conv_w[j], lru_conv_b[j],
                                 lru_gate_w[j], lru_gate_b[j], lru_lambda[j],
                                 lru_w_out[j], lru_b_out[j])
        else:
            mixed = stick_breaking_attention(hn, attn_w_qkv[j], attn_w_o[j])
        h = h + mixed
        h = h + swiglu_ffn(rms_norm(h, ffn_norm[layer]), ffn_w_in[layer], ffn_w_out[layer])
    return rms_norm(h, final_norm)


DEPTH_2 = 1

MOBA_HEADS = 8
MOBA_HEAD_DIM = 64
MOBA_BLOCK = 256
MOBA_TOPK = 3
MOBA_Q_CHUNK = 64
DIFF_HEADS = 4
DIFF_HEAD_DIM = 64
ATTN_Q_BLOCK = 128
ROPE_THETA = 10000.0
N_GROUPS = 4
EXPERTS_PER_GROUP = 8
N_EXPERTS = N_GROUPS * EXPERTS_PER_GROUP
EXPERT_TOPK = 2
D_EXPERT = 512
NORM_EPS = 1e-6
NEG_INF = -1e30
MOBA_WIDTH = MOBA_HEADS * MOBA_HEAD_DIM
DIFF_QK_WIDTH = DIFF_HEADS * 2 * DIFF_HEAD_DIM
DIFF_V_WIDTH = DIFF_HEADS * 2 * DIFF_HEAD_DIM
_SEGMENTS = (MOBA_WIDTH, MOBA_WIDTH, MOBA_WIDTH, DIFF_QK_WIDTH, DIFF_QK_WIDTH, DIFF_V_WIDTH, D_MODEL, D_MODEL)
IN_WIDTH = sum(_SEGMENTS)
IN_SPLITS = tuple(int(s) for s in np.cumsum(_SEGMENTS)[:-1])


def rmsnorm(x, g):
    xf = x.astype(jnp.float32)
    y = xf * lax.rsqrt(jnp.mean(xf * xf, axis=-1, keepdims=True) + NORM_EPS)
    return (y * g.astype(jnp.float32)).astype(x.dtype)

def rope_tables(seq, dim):
    inv = 1.0 / (ROPE_THETA ** (jnp.arange(0, dim, 2, dtype=jnp.float32) / dim))
    ang = jnp.arange(seq, dtype=jnp.float32)[:, None] * inv[None, :]
    return jnp.cos(ang), jnp.sin(ang)

def apply_rope(x, cos, sin):
    xf = x.astype(jnp.float32)
    half = x.shape[-1] // 2
    x1, x2 = xf[..., :half], xf[..., half:]
    return jnp.concatenate([x1 * cos - x2 * sin, x2 * cos + x1 * sin], axis=-1).astype(x.dtype)

def to_heads(t, n, d):
    b, s = t.shape[:2]
    return t.reshape(b, s, n, d).transpose(0, 2, 1, 3)

def moba_attention(q, k, v):
    B, H, S, dh = q.shape
    nb = -(-S // MOBA_BLOCK)
    topk = min(MOBA_TOPK, nb)
    pad = nb * MOBA_BLOCK - S
    kp = jnp.pad(k, ((0, 0), (0, 0), (0, pad), (0, 0)))
    vp = jnp.pad(v, ((0, 0), (0, 0), (0, pad), (0, 0)))
    k_blocks = kp.reshape(B, H, nb, MOBA_BLOCK, dh)
    v_blocks = vp.reshape(B, H, nb, MOBA_BLOCK, dh)
    k_mean = jnp.mean(k_blocks.astype(jnp.float32), axis=3)
    scale = dh ** -0.5
    nc = S // MOBA_Q_CHUNK
    q_chunks = q.reshape(B, H, nc, MOBA_Q_CHUNK, dh).transpose(2, 0, 1, 3, 4)
    starts = jnp.arange(nc, dtype=jnp.int32) * MOBA_Q_CHUNK
    b_idx = jnp.arange(B)[:, None, None, None]
    h_idx = jnp.arange(H)[None, :, None, None]
    block_ids = jnp.arange(nb, dtype=jnp.int32)
    own_offsets = jnp.arange(MOBA_BLOCK, dtype=jnp.int32)

    def chunk(args):
        qb, start = args
        blk = start // MOBA_BLOCK
        qpos = start + jnp.arange(MOBA_Q_CHUNK, dtype=jnp.int32)
        gate = jnp.einsum('bhqd,bhnd->bhqn', qb.astype(jnp.float32), k_mean)
        gate = jnp.where(block_ids < blk, gate, NEG_INF)
        _, sel = lax.top_k(gate, topk)
        valid = sel < blk
        ks = k_blocks[b_idx, h_idx, sel]
        vs = v_blocks[b_idx, h_idx, sel]
        s_sel = jnp.einsum('bhqd,bhqjnd->bhqjn', qb, ks).astype(jnp.float32) * scale
        s_sel = jnp.where(valid[..., None], s_sel, NEG_INF)
        s_sel = s_sel.reshape(B, H, MOBA_Q_CHUNK, topk * MOBA_BLOCK)
        k_own = lax.dynamic_slice_in_dim(kp, blk * MOBA_BLOCK, MOBA_BLOCK, axis=2)
        v_own = lax.dynamic_slice_in_dim(vp, blk * MOBA_BLOCK, MOBA_BLOCK, axis=2)
        s_own = jnp.einsum('bhqd,bhnd->bhqn', qb, k_own).astype(jnp.float32) * scale
        kpos = blk * MOBA_BLOCK + own_offsets
        s_own = jnp.where(kpos[None, :] <= qpos[:, None], s_own, NEG_INF)
        p = jax.nn.softmax(jnp.concatenate([s_sel, s_own], axis=-1), axis=-1).astype(v.dtype)
        p_sel = p[..., :topk * MOBA_BLOCK].reshape(B, H, MOBA_Q_CHUNK, topk, MOBA_BLOCK)
        p_own = p[..., topk * MOBA_BLOCK:]
        return (jnp.einsum('bhqjn,bhqjnd->bhqd', p_sel, vs)
                + jnp.einsum('bhqn,bhnd->bhqd', p_own, v_own))

    out = lax.map(chunk, (q_chunks, starts))
    return out.transpose(1, 2, 0, 3, 4).reshape(B, H, S, dh)

def diff_attention(q, k, v, lam):
    B, H2, S, dk = q.shape
    H = H2 // 2
    scale = dk ** -0.5
    nq = S // ATTN_Q_BLOCK
    q_blocks = q.reshape(B, H2, nq, ATTN_Q_BLOCK, dk).transpose(2, 0, 1, 3, 4)
    starts = jnp.arange(nq, dtype=jnp.int32) * ATTN_Q_BLOCK
    kpos = jnp.arange(S, dtype=jnp.int32)

    def block(args):
        qb, start = args
        s = jnp.einsum('bhqd,bhkd->bhqk', qb, k).astype(jnp.float32) * scale
        qpos = start + jnp.arange(ATTN_Q_BLOCK, dtype=jnp.int32)
        s = jnp.where(kpos[None, :] <= qpos[:, None], s, NEG_INF)
        p = jax.nn.softmax(s, axis=-1).reshape(B, H, 2, ATTN_Q_BLOCK, S)
        a = (p[:, :, 0] - lam * p[:, :, 1]).astype(v.dtype)
        return jnp.einsum('bhqk,bhkd->bhqd', a, v)

    out = lax.map(block, (q_blocks, starts))
    return out.transpose(1, 2, 0, 3, 4).reshape(B, H, S, 2 * dk)

def hierarchical_moe(h, w_group, b_group, w_expert, b_expert, w_gate, w_up, w_down):
    B, S, D = h.shape
    t = h.reshape(B * S, D)
    T = t.shape[0]
    g_prob = jax.nn.softmax((t @ w_group).astype(jnp.float32) + b_group, axis=-1)
    g_w, g_idx = lax.top_k(g_prob, 1)
    e_logits = ((t @ w_expert).astype(jnp.float32) + b_expert).reshape(T, N_GROUPS, EXPERTS_PER_GROUP)
    e_in_group = jnp.take_along_axis(e_logits, g_idx[:, :, None], axis=1)[:, 0]
    e_prob = jax.nn.softmax(e_in_group, axis=-1)
    e_w, e_idx = lax.top_k(e_prob, EXPERT_TOPK)
    e_w = e_w / jnp.sum(e_w, axis=-1, keepdims=True)
    weights = (g_w * e_w).reshape(-1)
    expert = (g_idx * EXPERTS_PER_GROUP + e_idx).reshape(-1)
    order = jnp.argsort(expert)
    tok = order // EXPERT_TOPK
    xs = t[tok]
    sizes = jnp.bincount(expert, length=N_EXPERTS).astype(jnp.int32)
    hid = jax.nn.silu(lax.ragged_dot(xs, w_gate, sizes)) * lax.ragged_dot(xs, w_up, sizes)
    out = lax.ragged_dot(hid.astype(xs.dtype), w_down, sizes)
    out = out * weights[order][:, None].astype(out.dtype)
    y = jnp.zeros_like(t).at[tok].add(out.astype(t.dtype))
    return y.reshape(B, S, D)

def second_inputs(seed: int = 0) -> dict:
    key = jax.random.key(seed)
    ks = jax.random.split(key, 24)
    D = D_MODEL

    def nrm(k, shape, scale):
        return jax.random.normal(k, shape, jnp.float32) * scale

    return {
        'x': nrm(ks[0], (BATCH, SEQ, D), 1.0),
        'c': nrm(ks[1], (BATCH, D), 1.0),
        'w_ada': nrm(ks[2], (DEPTH_2, D, 6 * D), 0.5 * D ** -0.5),
        'b_ada': nrm(ks[3], (DEPTH_2, 6 * D), 0.02),
        'norm1_g': 1.0 + nrm(ks[4], (DEPTH_2, D), 0.02),
        'w_in': nrm(ks[5], (DEPTH_2, D, IN_WIDTH), D ** -0.5),
        'lambda_q1': nrm(ks[6], (DEPTH_2, DIFF_HEAD_DIM), 0.1),
        'lambda_k1': nrm(ks[7], (DEPTH_2, DIFF_HEAD_DIM), 0.1),
        'lambda_q2': nrm(ks[8], (DEPTH_2, DIFF_HEAD_DIM), 0.1),
        'lambda_k2': nrm(ks[9], (DEPTH_2, DIFF_HEAD_DIM), 0.1),
        'diff_subln_g': 1.0 + nrm(ks[10], (DEPTH_2, 2 * DIFF_HEAD_DIM), 0.02),
        'w_proj_moba': nrm(ks[11], (DEPTH_2, MOBA_WIDTH, D), MOBA_WIDTH ** -0.5),
        'w_proj_diff': nrm(ks[12], (DEPTH_2, DIFF_V_WIDTH, D), DIFF_V_WIDTH ** -0.5),
        'w_out': nrm(ks[13], (DEPTH_2, D, D), D ** -0.5),
        'norm2_g': 1.0 + nrm(ks[14], (DEPTH_2, D), 0.02),
        'w_group': nrm(ks[15], (DEPTH_2, D, N_GROUPS), D ** -0.5),
        'b_group': nrm(ks[16], (DEPTH_2, N_GROUPS), 0.01),
        'w_expert': nrm(ks[17], (DEPTH_2, D, N_EXPERTS), D ** -0.5),
        'b_expert': nrm(ks[18], (DEPTH_2, N_EXPERTS), 0.01),
        'w_gate': nrm(ks[19], (DEPTH_2, N_EXPERTS, D, D_EXPERT), D ** -0.5),
        'w_up': nrm(ks[20], (DEPTH_2, N_EXPERTS, D, D_EXPERT), D ** -0.5),
        'w_down': nrm(ks[21], (DEPTH_2, N_EXPERTS, D_EXPERT, D), D_EXPERT ** -0.5),
        'final_g': 1.0 + nrm(ks[22], (D,), 0.02),
    }

def second_block(x, c, w_ada, b_ada, norm1_g, w_in, lambda_q1, lambda_k1, lambda_q2, lambda_k2,
              diff_subln_g, w_proj_moba, w_proj_diff, w_out, norm2_g, w_group, b_group,
              w_expert, b_expert, w_gate, w_up, w_down, final_g):
    S = x.shape[1]
    cos_m, sin_m = rope_tables(S, MOBA_HEAD_DIM)
    cos_d, sin_d = rope_tables(S, DIFF_HEAD_DIM)
    c_act = jax.nn.silu(c)
    for l in range(DEPTH_2):
        mod = c_act @ w_ada[l] + b_ada[l]
        sh1, sc1, g1, sh2, sc2, g2 = jnp.split(mod, 6, axis=-1)

        h = rmsnorm(x, norm1_g[l]) * (1.0 + sc1[:, None, :]) + sh1[:, None, :]
        proj = h @ w_in[l]
        q_m, k_m, v_m, q_d, k_d, v_d, gate_m, gate_d = jnp.split(proj, IN_SPLITS, axis=-1)

        qm = apply_rope(to_heads(q_m, MOBA_HEADS, MOBA_HEAD_DIM), cos_m, sin_m)
        km = apply_rope(to_heads(k_m, MOBA_HEADS, MOBA_HEAD_DIM), cos_m, sin_m)
        vm = to_heads(v_m, MOBA_HEADS, MOBA_HEAD_DIM)
        o_m = moba_attention(qm, km, vm)
        y_m = o_m.transpose(0, 2, 1, 3).reshape(x.shape[0], S, MOBA_WIDTH) @ w_proj_moba[l]

        lam_init = 0.8 - 0.6 * math.exp(-0.3 * l)
        lam = (jnp.exp(jnp.sum(lambda_q1[l].astype(jnp.float32) * lambda_k1[l].astype(jnp.float32)))
               - jnp.exp(jnp.sum(lambda_q2[l].astype(jnp.float32) * lambda_k2[l].astype(jnp.float32)))
               + lam_init)
        qd = apply_rope(to_heads(q_d, 2 * DIFF_HEADS, DIFF_HEAD_DIM), cos_d, sin_d)
        kd = apply_rope(to_heads(k_d, 2 * DIFF_HEADS, DIFF_HEAD_DIM), cos_d, sin_d)
        vd = to_heads(v_d, DIFF_HEADS, 2 * DIFF_HEAD_DIM)
        o_d = diff_attention(qd, kd, vd, lam)
        o_d = rmsnorm(o_d, diff_subln_g[l]) * (1.0 - lam_init)
        y_d = o_d.transpose(0, 2, 1, 3).reshape(x.shape[0], S, DIFF_V_WIDTH) @ w_proj_diff[l]

        merged = jax.nn.sigmoid(gate_m) * y_m + jax.nn.sigmoid(gate_d) * y_d
        x = x + g1[:, None, :] * (merged @ w_out[l])

        h2 = rmsnorm(x, norm2_g[l]) * (1.0 + sc2[:, None, :]) + sh2[:, None, :]
        y_ffn = hierarchical_moe(h2, w_group[l], b_group[l], w_expert[l], b_expert[l],
                                 w_gate[l], w_up[l], w_down[l])
        x = x + g2[:, None, :] * y_ffn
    return rmsnorm(x, final_g)


def setup_inputs(seed=0):
    out = dict(first_inputs(seed))
    for name, value in second_inputs(seed + 1).items():
        if name != "x":
            out[name + "_2"] = value
    return out


def reference(
    x, mix_norm, ffn_norm, final_norm, lru_w_in, lru_b_in, lru_conv_w, lru_conv_b, lru_gate_w,
    lru_gate_b, lru_lambda, lru_w_out, lru_b_out, attn_w_qkv, attn_w_o, ffn_w_in, ffn_w_out,
    c_2, w_ada_2, b_ada_2, norm1_g_2, w_in_2, lambda_q1_2, lambda_k1_2, lambda_q2_2,
    lambda_k2_2, diff_subln_g_2, w_proj_moba_2, w_proj_diff_2, w_out_2, norm2_g_2, w_group_2,
    b_group_2, w_expert_2, b_expert_2, w_gate_2, w_up_2, w_down_2, final_g_2,
):
    x = first_block(
        x, mix_norm, ffn_norm, final_norm, lru_w_in, lru_b_in, lru_conv_w, lru_conv_b,
        lru_gate_w, lru_gate_b, lru_lambda, lru_w_out, lru_b_out, attn_w_qkv, attn_w_o,
        ffn_w_in, ffn_w_out,
    )
    return second_block(
        x, c_2, w_ada_2, b_ada_2, norm1_g_2, w_in_2, lambda_q1_2, lambda_k1_2, lambda_q2_2,
        lambda_k2_2, diff_subln_g_2, w_proj_moba_2, w_proj_diff_2, w_out_2, norm2_g_2,
        w_group_2, b_group_2, w_expert_2, b_expert_2, w_gate_2, w_up_2, w_down_2, final_g_2,
    )


_drawn_inputs = setup_inputs


def setup_inputs(seed=0):
    import zlib

    import numpy as np

    out = dict(_drawn_inputs(seed))
    spreads = {}
    factors = {'lru_gate_b': 8.0,
     'b_ada_2': 3.224,
     'norm1_g_2': 8.0,
     'lambda_q1_2': 8.0,
     'lambda_k1_2': 8.0,
     'lambda_k2_2': 8.0,
     'diff_subln_g_2': 8.0,
     'norm2_g_2': 5.242,
     'b_group_2': 7.684,
     'b_expert_2': 8.0,
     'final_g_2': 2.949}
    for name, (base, spread) in spreads.items():
        noise = np.random.default_rng([zlib.crc32(name.encode()), seed]).standard_normal(out[name].shape)
        drawn = base * np.exp(spread * noise) if base else spread * noise
        out[name] = jnp.asarray(drawn.astype(out[name].dtype))
    for name, factor in factors.items():
        out[name] = (out[name] * factor).astype(out[name].dtype)
    return out
```

```python
from contextlib import ExitStack

import numpy as np

import concourse.bass as bass
from concourse import mybir

F32 = mybir.dt.float32
I32 = mybir.dt.int32
ALU = mybir.AluOpType
ACT = mybir.ActivationFunctionType
AX_X = mybir.AxisListType.X

P = 128
SEQ = 256
D = 1024
KC = D // P
TC = SEQ // P
D_FF = 2816
FFN_COLS = 256
FFN_STEPS = D_FF // FFN_COLS
HEADS = 16
HD = 64
N_EXP, N_GRP, GRP = 32, 4, 8
D_EXP = 512
EC = D_EXP // P
SLOTS = 2 * SEQ
SC = SLOTS // P
WIN = 64
SLOT_PAD = SLOTS + WIN
EPS = 1e-6
SCALE = HD ** -0.5
NEG = -1e30
LAM_INIT = 0.2
HALF = KC // 2

C_ID, C_AFTER, C_BEFORE, C_ONES, C_ROT, C_STICK, C_NEG = 0, 128, 256, 384, 512, 640, 1024
C_IOTA = 1408
N_CONST = C_IOTA + GRP

R_MIX, R_FFN, R_BIN, R_CW, R_CB, R_GB, R_LAM, R_BOUT, R_FIN1, N_ROWS_A = 0, 16, 32, 48, 80, 88, 104, 112, 120, 128
R_N1, R_N2, R_FIN, R_ADA, R_SUB, R_C, N_ROWS_B = 0, 8, 16, 24, 72, 73, 81

UNITS = ([f"rec{i}" for i in range(2)] + [f"gb{i}" for i in range(2)] + ["gates"] + [f"lo{i}" for i in range(2)]
         + [f"ffn0_{i}" for i in range(FFN_STEPS)]
         + ["q0", "q1", "k0", "k1", "v0", "v1", "wo0", "wo1"]
         + [f"ffn1_{i}" for i in range(FFN_STEPS)]
         + ["qm", "km", "vm", "qd", "kd", "vd", "gm0", "gm1", "gd0", "gd1", "pm", "pd", "out0", "out1"])
UNIT = 4096
FFN_UNIT = 6144
RING_A = 3 * UNIT
EXPERT = 3 * UNIT
UNIT_NO = {n: i for i, n in enumerate(UNITS)}

TILES = ([f"rec{i}" for i in range(4)] + [f"gb{i}" for i in range(4)] + [f"gate{n}_{g}" for n in range(4) for g in range(2)]
         + [f"q{i}" for i in range(4)] + [f"k{i}" for i in range(4)] + [f"v{i}" for i in range(4)]
         + ["qm0", "qm1", "km0", "km1", "vm0", "vm1", "qd0", "qd1", "kd0", "kd1", "vd0", "vd1"]
         + [f"rot{i}" for i in range(8)]
         + [f"gm{i}" for i in range(4)] + [f"gd{i}" for i in range(4)]
         + [f"ym{i}" for i in range(4)] + [f"yd{i}" for i in range(4)])
TILE_NO = {n: i for i, n in enumerate(TILES)}

SUMMED = [n for n in UNITS if n[:2] in ("lo", "wo") or n[:3] in ("ffn", "out")]
LAST_TILE = {"rec0": "rec1", "rec1": "rec3", "gb0": "gb1", "gb1": "gb3", "gates": "gate3_1", "q0": "q1", "q1": "q3", "k0": "k1",
             "k1": "k3", "v0": "v1", "v1": "v3", "qm": "qm1", "km": "km1", "vm": "vm1", "qd": "qd1", "kd": "kd1", "vd": "vd1",
             "gm0": "gm1", "gm1": "gm3", "gd0": "gd1", "gd1": "gd3", "pm": "ym3", "pd": "yd3"}


def summed_by(name):
    return SUMMED.index(name) + 1


def ring_places():
    places, at, previous = [], 0, None
    for name in UNITS:
        size = FFN_UNIT if name.startswith("ffn") else UNIT
        if size != previous or at + size > RING_A:
            at = 0
        places.append((at, size))
        at, previous = at + size, size
    before = []
    for n, (a, s) in enumerate(places):
        clash = [m for m in range(n) if places[m][0] < a + s and a < places[m][0] + places[m][1]]
        before.append(UNITS[max(clash)] if clash else None)
    return places, before


def program(nc, a, out):
    places, unit_before = ring_places()
    with ExitStack() as ctx:
        def sb(name, shape, dt=F32):
            return ctx.enter_context(nc.sbuf_tensor(name, shape, dt))

        def sem(name):
            return ctx.enter_context(nc.semaphore(name))

        ring_a = sb("ring_a", [P, RING_A])
        ring_b = sb("ring_b", [P, 2 * EXPERT])
        xT = sb("xT", [P, KC, SEQ])
        big = sb("big", [P, 2048 + 9728])
        cst = sb("cst", [P, N_CONST])
        cols = sb("cols", [P, N_ROWS_A + N_ROWS_B])
        rstd = sb("rstd", [P, SEQ])
        ada = sb("ada", [P, 48])
        gain = sb("gain", [P, 2, KC])
        small = sb("small", [P, 400])
        bias36 = sb("bias36", [P, N_GRP + N_EXP])
        info = sb("info", [1, 3 * N_EXP], I32)
        ps = ctx.enter_context(nc.psum_tensor("ps", [P, 8, 512], F32))

        ident = cst[:, C_ID:C_ID + P]
        after = cst[:, C_AFTER:C_AFTER + P]
        before = cst[:, C_BEFORE:C_BEFORE + P]
        ones = cst[:, C_ONES:C_ONES + P]
        rot = cst[:, C_ROT:C_ROT + P]
        stick = cst[:, C_STICK:C_STICK + 384]
        negm = cst[:, C_NEG:C_NEG + 384]
        iota8 = cst[:, C_IOTA:C_IOTA + GRP]

        def flat(lo, n):
            return big[:, lo:lo + n]

        def fm(lo, k=KC):
            return flat(lo, k * SEQ).rearrange("p (k t) -> p k t", k=k)

        hT = fm(0)
        WORK = 2048
        rec = flat(WORK, KC * (SEQ + 3)).rearrange("p (k t) -> p k t", k=KC)
        tb = fm(WORK)
        cv = fm(WORK + 2080)
        gl = fm(WORK + 2080 + 2048)
        ib = fm(WORK + 2080 + 4096)
        xtok = flat(WORK + 2080 + 4096, 2048).rearrange("p (c f) -> p c f", c=TC)
        rows_a = flat(WORK, P)
        rows_b = flat(WORK + P, P)
        qT, kT = fm(WORK), fm(WORK + 2048)
        vtok = flat(WORK + 4096, 2048).rearrange("p (c f) -> p c f", c=TC)
        sk = flat(WORK + 6144, 6 * 512).rearrange("p (b n) -> p b n", b=6)
        sk_e, sk_p, sk_t = ([sk[:, 2 * i + b, 0:384] for b in range(2)] for i in range(3))
        hid = flat(WORK, 2 * 512).rearrange("p (b n) -> p b n", b=2)
        qm, km = fm(WORK, 4), fm(WORK + 1024, 4)
        vm = flat(WORK + 2048, 1024).rearrange("p (c f) -> p c f", c=TC)
        gd = fm(WORK + 1024)
        qd, kd = fm(WORK + 3072, 4), fm(WORK + 4096, 4)
        vd = flat(WORK + 5120, 1024).rearrange("p (c f) -> p c f", c=TC)
        gm = fm(WORK + 6144)
        TMP = WORK + 8192
        rope = flat(TMP, 512)
        rope_t = flat(TMP + 512, 512)
        rope_u = flat(TMP + 1024, 512)
        ada_acc = flat(WORK + 6144, 1024).rearrange("p (b n) -> p b n", b=2)
        pbuf = [flat(TMP + 384 * i, 384) for i in range(2)]
        ptb = [flat(TMP + 768 + 384 * i, 384) for i in range(2)]
        h2tok = flat(2048, 2048).rearrange("p (c f) -> p c f", c=TC)
        pick = flat(4096, 1024).rearrange("p (c s) -> p c s", c=TC)
        slot_no = flat(5120, SLOTS)
        pick_t = flat(5632, SLOTS)
        xs = flat(5120, KC * SLOT_PAD).rearrange("p (k s) -> p k s", k=KC)
        ys = flat(0, KC * SLOT_PAD).rearrange("p (k s) -> p k s", k=KC)
        combT = flat(9728, SC * SEQ).rearrange("p (s t) -> p s t", s=SC)
        comb = flat(10752, 1024).rearrange("p (c s) -> p c s", c=TC)
        hidE = flat(10752, D_EXP)[0:WIN]
        xw = flat(11264, KC * WIN).rearrange("p (k s) -> p k s", k=KC)
        hidT = flat(KC * SLOT_PAD, EC * WIN).rearrange("p (k s) -> p k s", k=EC)
        yE = [hidE, cst[0:WIN, C_STICK:C_STICK + 512]]
        ystok = flat(5120, SC * D).rearrange("p (s f) -> p s f", s=SC)
        otok = flat(2048, 2048).rearrange("p (c f) -> p c f", c=TC)
        w_route = flat(WORK + 9728 - KC * 36, KC * 36).rearrange("p (k n) -> p k n", k=KC)

        def col(row, table=0):
            i = row + (N_ROWS_A if table else 0)
            return cols[:, i:i + 1]

        a_loaded = [sem(f"a_loaded{i}") for i in range(3)]
        fi_loaded = [sem(f"fi_loaded{i}") for i in range(2)]
        fo_loaded = [sem(f"fo_loaded{i}") for i in range(2)]
        unit_summed = sem("unit_summed")
        ada_loaded = [sem(f"ada_loaded{i}") for i in range(6)]
        ada_used = sem("ada_used")
        ada_psum = sem("ada_psum")
        gates_in = sem("gates_in")
        const_in, rows_in, xtok_in, rope_in, route_in = (sem(n) for n in ("const_in", "rows_in", "xtok_in", "rope_in", "route_in"))
        slotno_in = sem("slotno_in")
        lam_in = sem("lam_in")
        tile_done = sem("tile_done")
        evac = [sem(f"evac{b}") for b in range(4)]
        setup_pe, setup_ev = sem("setup_pe"), sem("setup_ev")
        x_ready = sem("x_ready")
        sq_done, sum_done, ms_done, root_done = (sem(n) for n in ("sq_done", "sum_done", "ms_done", "root_done"))
        h_part, h_ready = sem("h_part"), sem("h_ready")
        dve_ch, act_ch = sem("dve_ch"), sem("act_ch")
        pad_zero = sem("pad_zero")
        sp8_ready = sem("sp8_ready")
        conv_done, gate_sum, ta_done, ratio_done, mult_done, y_done = (
            sem(n) for n in ("conv_done", "gate_sum", "ta_done", "ratio_done", "mult_done", "y_done"))
        ffn_gu, ffn_silu, ffn_hid = sem("ffn_gu"), sem("ffn_silu"), sem("ffn_hid")
        z_done, soft_done, spm_done, z_read, suf_done, arg_done, w_exp, w_done, o_done, o_evac = (
            sem(n) for n in ("z_done", "soft_done", "spm_done", "z_read", "suf_done", "arg_done", "w_exp", "w_done", "o_done", "o_evac"))
        mod_ready = sem("mod_ready")
        roped = sem("roped")
        s_done, s_max, p_exp, p_norm, t_done, pt_evac, av_done, av_evac = (
            sem(n) for n in ("s_done", "s_max", "p_exp", "p_norm", "t_done", "pt_evac", "av_done", "av_evac"))
        osq_done, osum_done, oms_done, oroot_done, on_ready = (
            sem(n) for n in ("osq_done", "osum_done", "oms_done", "oroot_done", "on_ready"))
        merged_ready = sem("merged_ready")
        logit_done, gexp_done, gmax_done, e2_done, m2_ready, mask_ready, pos_done = (
            sem(n) for n in ("logit_done", "gexp_done", "gmax_done", "e2_done", "m2_ready", "mask_ready", "pos_done"))
        htok_pe, htok_ev, pick_ready, comb_ready, gather_pe, gather_ev, combT_pe, combT_ev = (
            sem(n) for n in ("htok_pe", "htok_ev", "pick_ready", "comb_ready", "gather_pe", "gather_ev", "combT_pe", "combT_ev"))
        info_ready = sem("info_ready")
        gu_used = sem("gu_used")
        xw_ready = sem("xw_ready")
        gu_loaded = [sem(f"gu_loaded{i}") for i in range(3)]
        dn_loaded = [sem(f"dn_loaded{i}") for i in range(3)]
        expert_used = sem("expert_used")
        gu_done, silu_done, hid_done, hidT_pe, hidT_ev, down_done, y_ev = (
            [sem(f"{n}{h}") for h in range(2)] for n in ("gu_done", "silu_done", "hid_done", "hidT_pe", "hidT_ev", "down_done", "y_ev"))
        ywin_pe, win_evac = sem("ywin_pe"), sem("win_evac")
        yt_pe, yt_act, yt_dve, y2_done, fin_pe, fin_ev, stored = (
            sem(n) for n in ("yt_pe", "yt_act", "yt_dve", "y2_done", "fin_pe", "fin_ev", "stored"))

        def unit_view(name):
            at, _ = places[UNIT_NO[name]]
            v = ring_a[:, at:at + UNIT]
            if name == "gates":
                return v.rearrange("p (g n c d) -> p g n c d", g=2, n=4, c=2)
            if name[:2] in ("lo", "wo", "pm", "pd") or name[:3] == "out":
                return v.rearrange("p (k f) -> p k f", k=4)
            return v.rearrange("p (k f) -> p k f", k=KC)

        def ffn_views(slot):
            v = ring_a[:, slot * FFN_UNIT:(slot + 1) * FFN_UNIT]
            return (v[:, 0:2048].rearrange("p (k f) -> p k f", k=KC), v[:, 2048:4096].rearrange("p (k f) -> p k f", k=KC),
                    v[:, 4096:6144].rearrange("p (k f) -> p k f", k=2))

        def unit_source(name):
            def columns(w, c):
                return w[:, c * 512:(c + 1) * 512].rearrange("(k p) n -> p k n", p=P)

            def krows(w, c):
                return w[c * 512:(c + 1) * 512, :].rearrange("(k p) n -> p k n", p=P)

            i = int(name[-1]) if name[-1].isdigit() else 0
            if name.startswith("rec"):
                return columns(a["lru_w_in"][0], 2 + i)
            if name.startswith("gb"):
                return columns(a["lru_w_in"][0], i)
            if name.startswith("lo"):
                return krows(a["lru_w_out"][0], i)
            if name.startswith("wo"):
                return krows(a["attn_w_o"][0], i)
            if name.startswith("out"):
                return krows(a["w_out_2"][0], i)
            if name == "pm":
                return krows(a["w_proj_moba_2"][0], 0)
            if name == "pd":
                return krows(a["w_proj_diff_2"][0], 0)
            if name in ("q0", "q1", "k0", "k1", "v0", "v1"):
                return columns(a["attn_w_qkv"][0], 2 * "qkv".index(name[0]) + i)
            return columns(a["w_in_2"][0], ["qm", "km", "vm", "qd", "kd", "vd", "gm0", "gm1", "gd0", "gd1"].index(name))

        load_count = {}
        for name in UNITS:
            if not name.startswith("ffn"):
                s = places[UNIT_NO[name]][0] // UNIT
                load_count[name] = (s, 1 + sum(1 for m in load_count if load_count[m][0] == s and m != "gates"))

        def wait_unit(eng, name):
            s, n = load_count[name]
            eng.wait_ge(a_loaded[s], 16 * n)

        def wait_used(eng, name):
            if name in SUMMED:
                eng.wait_ge(unit_summed, summed_by(name))
            else:
                eng.wait_ge(tile_done, TILE_NO[LAST_TILE[name]] + 1)

        def wait_tile(eng, name):
            eng.wait_ge(tile_done, TILE_NO[name] + 1)

        def wait_evac(eng, name):
            t = TILE_NO[name]
            eng.wait_ge(evac[t % 4], t // 4 + 1)

        def bank(name):
            return ps[:, TILE_NO[name] % 4, :]

        def evac_sem(name):
            return evac[TILE_NO[name] % 4]

        def expert_place(e3):
            v = ring_a[:, 0:EXPERT] if e3 == 2 else ring_b[:, e3 * EXPERT:(e3 + 1) * EXPERT]
            return (v[:, 0:UNIT].rearrange("p (k f) -> p k f", k=KC), v[:, UNIT:2 * UNIT].rearrange("p (k f) -> p k f", k=KC),
                    v[:, 2 * UNIT:].rearrange("p (k f) -> p k f", k=EC))

        def window(buf, start, w):
            at = nc.s_assert_within(start + w * WIN, 0, SLOTS, skip_runtime_bounds_check_because="w * WIN is less than the expert's slots, which end by SLOTS, or w is 0")
            return buf[:, bass.ds(at, WIN)] if len(buf.shape) == 2 else buf[:, :, bass.ds(at, WIN)]

        def load_expert(eng, e, e3, gu_free=None, dn_free=None):
            g, u, dn = expert_place(e3)
            if gu_free is not None:
                eng.wait_ge(gu_used, gu_free)
            eng.dma_start(g, a["w_gate_2"][0, bass.ds(e, 1)].rearrange("e (k p) f -> p (e k) f", p=P)).then_inc(gu_loaded[e3], 16)
            eng.dma_start(u, a["w_up_2"][0, bass.ds(e, 1)].rearrange("e (k p) f -> p (e k) f", p=P)).then_inc(gu_loaded[e3], 16)
            if dn_free is not None:
                eng.wait_ge(expert_used, dn_free)
            eng.dma_start(dn, a["w_down_2"][0, bass.ds(e, 1)].rearrange("e (k p) f -> p (e k) f", p=P)).then_inc(dn_loaded[e3], 16)

        block = ctx.enter_context(nc.Block())

        @block.sync
        def _(sp):
            sp.dma_start(xtok, a["x"][0].rearrange("(c p) f -> p c f", p=P)).then_inc(xtok_in, 16)

            def load_unit(name):
                n = UNIT_NO[name]
                if unit_before[n]:
                    wait_used(sp, unit_before[n])
                s, _ = load_count[name]
                dst = unit_view(name)
                if name == "gates":
                    for g in range(2):
                        for b in range(4):
                            ins = sp.dma_start(dst[:, g, b], a["lru_gate_w"][0, g, b].rearrange("(c p) d -> p c d", p=P))
                            ins.then_inc(gates_in, 16)
                    return
                sp.dma_start(dst, unit_source(name)).then_inc(a_loaded[s], 16)

            def load_ffn(layer, i, slot, gu_free=None, dn_free=None):
                g, u, dn = ffn_views(slot)
                if gu_free is not None:
                    sp.wait_ge(ffn_gu, gu_free)
                w_in, w_out = a["ffn_w_in"][layer], a["ffn_w_out"][layer]
                sp.dma_start(g, w_in[:, bass.ds(i * FFN_COLS, FFN_COLS)].rearrange("(k p) n -> p k n", p=P)).then_inc(fi_loaded[slot], 16)
                sp.dma_start(u, w_in[:, bass.ds(i * FFN_COLS + D_FF, FFN_COLS)].rearrange("(k p) n -> p k n", p=P)).then_inc(fi_loaded[slot], 16)
                if dn_free is not None:
                    sp.wait_ge(unit_summed, dn_free)
                sp.dma_start(dn, w_out[bass.ds(i * FFN_COLS, FFN_COLS), :].rearrange("(k p) n -> p k n", p=P)).then_inc(fo_loaded[slot], 16)

            def load_ffn_layer(layer):
                base = summed_by(f"ffn{layer}_0")
                for i in range(2):
                    wait_used(sp, unit_before[UNIT_NO[f"ffn{layer}_{i}"]])
                    load_ffn(layer, i, i)
                gu = layer * FFN_STEPS + 1
                with sp.Fori(0, (FFN_STEPS - 3) // 2) as j:
                    for i in range(2):
                        load_ffn(layer, 2 * j + 2 + i, i, 2 * j + gu + i, 2 * j + base + i)
                load_ffn(layer, FFN_STEPS - 1, 0, gu + FFN_STEPS - 3, base + FFN_STEPS - 3)

            for name in UNITS:
                if name.startswith("ffn"):
                    if name.endswith("_0"):
                        load_ffn_layer(int(name[3]))
                    continue
                load_unit(name)
                if name in ("wo1", "qm"):
                    sp.wait_ge(ada_used, 12)
                    load_expert(sp, int(name == "qm"), int(name == "qm"))
                if name == "kd":
                    sp.wait_ge(h_ready, 4)
                    sp.dma_start(rope, a["rope"]).then_inc(rope_in, 16)
            wait_used(sp, "out1")
            load_expert(sp, 2, 2)
            with sp.Fori(0, (N_EXP - 5) // 3) as j:
                for s in range(3):
                    load_expert(sp, 3 * j + 3 + s, s, 3 * j + s + 1, 3 * j + s + 1)
            for e in range(3 + 3 * ((N_EXP - 5) // 3), N_EXP):
                load_expert(sp, e, e % 3, e - 2, e - 2)
            sp.wait_ge(fin_ev, 4)
            sp.dma_start(out[0].rearrange("(c p) f -> p c f", p=P), otok).then_inc(stored, 16)
            sp.wait_ge(stored, 16)

        @block.gpsimd
        def _(pool):
            rows = [
                (rows_a, R_MIX, a["mix_norm"].rearrange("l (k p) -> (l k) p", p=P)),
                (rows_a, R_FFN, a["ffn_norm"].rearrange("l (k p) -> (l k) p", p=P)),
                (rows_a, R_BIN, a["lru_b_in"].rearrange("l (k p) -> (l k) p", p=P)),
                (rows_a, R_CW, a["lru_conv_w"][0].rearrange("w (k p) -> (w k) p", p=P)),
                (rows_a, R_CB, a["lru_conv_b"].rearrange("l (k p) -> (l k) p", p=P)),
                (rows_a, R_GB, a["lru_gate_b"][0].rearrange("g (k p) -> (g k) p", p=P)),
                (rows_a, R_LAM, a["lru_lambda"].rearrange("l (k p) -> (l k) p", p=P)),
                (rows_a, R_BOUT, a["lru_b_out"].rearrange("l (k p) -> (l k) p", p=P)),
                (rows_a, R_FIN1, a["final_norm"].rearrange("(k p) -> k p", p=P)),
                (rows_b, R_N1, a["norm1_g_2"].rearrange("l (k p) -> (l k) p", p=P)),
                (rows_b, R_N2, a["norm2_g_2"].rearrange("l (k p) -> (l k) p", p=P)),
                (rows_b, R_FIN, a["final_g_2"].rearrange("(k p) -> k p", p=P)),
                (rows_b, R_ADA, a["b_ada_2"].rearrange("l (k p) -> (l k) p", p=P)),
                (rows_b, R_SUB, a["diff_subln_g_2"]),
                (rows_b, R_C, a["c_2"].rearrange("l (k p) -> (l k) p", p=P)),
            ]
            pool.dma_start(cst[:], a["constants"]).then_inc(const_in, 16)
            for dst, r, src in rows:
                pool.dma_start(dst[r:r + src.shape[0], :], src).then_inc(rows_in, 16)
            pool.dma_start(bias36[:, 0:N_GRP], a["b_group_2"].to_broadcast([P, N_GRP])).then_inc(lam_in, 16)
            pool.dma_start(bias36[:, N_GRP:], a["b_expert_2"].to_broadcast([P, N_EXP])).then_inc(lam_in, 16)
            for i, n in enumerate(("lambda_q1_2", "lambda_k1_2", "lambda_q2_2", "lambda_k2_2")):
                pool.dma_start(small[:, i * HD:(i + 1) * HD], a[n].to_broadcast([P, HD])).then_inc(lam_in, 16)
            for u in range(12):
                if u >= 6:
                    pool.wait_ge(ada_used, u - 5)
                dst = ring_b[:, (u % 6) * UNIT:(u % 6 + 1) * UNIT].rearrange("p (k f) -> p k f", k=KC)
                pool.dma_start(dst, a["w_ada_2"][0][:, u * 512:(u + 1) * 512].rearrange("(k p) n -> p k n", p=P)).then_inc(ada_loaded[u % 6], 16)
            for h in range(HEADS):
                pool.wait_ge(w_exp, h + 1)
                nc.gpsimd.tensor_tensor(sk_e[h % 2], sk_e[h % 2], stick, ALU.mult).then_inc(w_done, 1)
            pool.wait_ge(x_ready, 7)
            pool.dma_start(w_route[:, :, 0:N_GRP], a["w_group_2"][0].rearrange("(k p) n -> p k n", p=P)).then_inc(route_in, 16)
            pool.dma_start(w_route[:, :, N_GRP:], a["w_expert_2"][0].rearrange("(k p) n -> p k n", p=P)).then_inc(route_in, 16)
            pool.dma_start(slot_no, a["slot_numbers"]).then_inc(slotno_in, 16)
            pool.wait_ge(gather_ev, KC + 1)
            pool.wait_ge(combT_ev, 2)
            pool.wait_ge(info_ready, 1)
            with pool.Fori(0, N_EXP) as e:
                start = pool.value_load(info[0:1, bass.ds(e, 1)], min_val=0, max_val=SLOTS)
                n_win = pool.value_load(info[0:1, bass.ds(e + N_EXP, 1)], min_val=1, max_val=SEQ // WIN)
                first = pool.value_load(info[0:1, bass.ds(e + 2 * N_EXP, 1)], min_val=0, max_val=N_EXP + SLOTS // WIN)
                with pool.Fori(0, n_win) as w:
                    pool.wait_ge(gu_done[1], first + w + 1)
                    nc.gpsimd.tensor_copy(xw, window(xs, start, w)).then_inc(xw_ready, 1)

        @block.scalar
        def _(act):
            n_chain = [0]

            def link(ins):
                n_chain[0] += 1
                ins.then_inc(act_ch, 1)
                act.wait_ge(act_ch, n_chain[0])

            def norm_square(n):
                act.wait_ge(x_ready, n + 1)
                nc.scalar.activation(hT, xT[:], ACT.Square).then_inc(sq_done, 1)

            def norm_root(n):
                act.wait_ge(ms_done, n + 1)
                nc.scalar.activation(rstd[:], rstd[:], ACT.Sqrt).then_inc(root_done, 1)

            def norm_shift(n, shift):
                for k in range(KC):
                    act.wait_ge(h_part, KC * (n - 5) + k + 1)
                    ins = nc.scalar.activation(hT[:, k], hT[:, k], ACT.Identity, bias=ada[:, shift + k:shift + k + 1])
                ins.then_inc(h_ready, 1)

            def copy_pair(name, dst, func=ACT.Copy):
                wait_tile(act, name)
                nc.scalar.activation(dst, bank(name), func).then_inc(evac_sem(name), 1)

            lam = cols[:, R_LAM:R_LAM + 8]
            act.wait_ge(setup_ev, 2)
            nc.scalar.activation(small[:, 256:264], cols[:, N_ROWS_A + R_C:N_ROWS_A + R_C + 8], ACT.Silu).then_inc(mod_ready, 1)
            link(nc.scalar.activation(small[:, 272:280], lam, ACT.Abs))
            link(nc.scalar.activation(small[:, 272:280], small[:, 272:280], ACT.Exp, scale=-1.0))
            nc.scalar.activation(small[:, 272:280], small[:, 272:280], ACT.Ln, bias=1.0).then_inc(sp8_ready, 1)

            norm_square(0)
            norm_root(0)
            act.wait_ge(pad_zero, 1)
            for i in range(4):
                wait_tile(act, f"rec{i}")
                for d in range(2):
                    m = 2 * i + d
                    ins = nc.scalar.activation(rec[:, m, 3:], bank(f"rec{i}")[:, d * 256:(d + 1) * 256], ACT.Identity, bias=col(R_BIN + 8 + m))
                ins.then_inc(evac_sem(f"rec{i}"), 1)
            for i in range(4):
                wait_tile(act, f"gb{i}")
                for d in range(2):
                    m = 2 * i + d
                    ins = nc.scalar.activation(gl[:, m], bank(f"gb{i}")[:, d * 256:(d + 1) * 256], ACT.Gelu_apprx_tanh, bias=col(R_BIN + m))
                ins.then_inc(evac_sem(f"gb{i}"), 1)
            for n in range(4):
                for g in range(2):
                    name = f"gate{n}_{g}"
                    wait_tile(act, name)
                    for d in range(2):
                        m = 2 * n + d
                        dst = (hT, ib)[g][:, m]
                        ins = nc.scalar.activation(dst, bank(name)[:, d * 256:(d + 1) * 256], ACT.Sigmoid, bias=col(R_GB + 8 * g + m))
                    ins.then_inc(evac_sem(name), 1)
            act.wait_ge(sp8_ready, 2)
            act.wait_ge(conv_done, 2)
            wait_evac(act, "gate3_0")
            for hf in range(2):
                for m in range(HALF * hf, HALF * hf + HALF):
                    nc.scalar.activation(tb[:, m], hT[:, m], ACT.Tanh, scale=small[:, 280 + m:281 + m])
                    ins = nc.scalar.activation(hT[:, m], hT[:, m], ACT.Exp, scale=small[:, 288 + m:289 + m])
                ins.then_inc(ta_done, 1)
            for hf in range(2):
                act.wait_ge(ratio_done, hf + 1)
                half = tb[:, HALF * hf:HALF * hf + HALF]
                nc.scalar.activation(half, half, ACT.Sqrt, scale=2.0).then_inc(mult_done, 1)

            def ffn(layer):
                def silu(slot, step):
                    act.wait_ge(ffn_gu, step + 1)
                    nc.scalar.activation(hid[:, slot], ps[:, 2 * slot, :], ACT.Silu).then_inc(ffn_silu, 1)

                base = layer * FFN_STEPS
                silu(0, base)
                for s in range(1, 3):
                    silu(s % 2, base + s)
                with act.Fori(0, (FFN_STEPS - 3) // 2) as j:
                    silu(1, 2 * j + base + 3)
                    silu(0, 2 * j + base + 4)

            norm_square(1)
            norm_root(1)
            ffn(0)

            norm_square(2)
            norm_root(2)
            for nm, dst in (("q", qT), ("k", kT)):
                for i in range(4):
                    copy_pair(f"{nm}{i}", dst[:, 2 * i:2 * i + 2])
            for i in range(4):
                copy_pair(f"v{i}", vtok[:, i % 2, (i // 2) * 512:(i // 2 + 1) * 512])

            def soft(h):
                b = h % 2
                act.wait_ge(z_done, h + 1)
                if h >= 2:
                    act.wait_ge(o_done, h - 1)
                link(nc.scalar.activation(sk_e[b], ps[:, b, 0:384], ACT.Abs, scale=SCALE))
                link(nc.scalar.activation(sk_e[b], sk_e[b], ACT.Exp, scale=-1.0))
                nc.scalar.activation(sk_e[b], sk_e[b], ACT.Ln, bias=1.0).then_inc(soft_done, 1)

            def weights(h):
                act.wait_ge(arg_done, h + 1)
                nc.scalar.activation(sk_e[h % 2], sk_t[h % 2], ACT.Exp).then_inc(w_exp, 1)

            def o_copy(c):
                act.wait_ge(o_done, 2 * c + 2)
                nc.scalar.activation(hT[:, c], ps[:, 4 + c % 2, 0:256], ACT.Copy).then_inc(o_evac, 1)

            soft(0)
            for h in range(HEADS):
                if h + 1 < HEADS:
                    soft(h + 1)
                weights(h)
                if h % 2 == 1 and h >= 3:
                    o_copy(h // 2 - 1)
            o_copy(7)
            norm_square(3)
            norm_root(3)
            ffn(1)

            norm_square(4)
            norm_root(4)
            norm_square(5)
            norm_root(5)
            norm_shift(5, 0)
            copy_pair("qm0", qm[:, 0:2])
            copy_pair("qm1", qm[:, 2:4])
            copy_pair("km0", km[:, 0:2])
            copy_pair("km1", km[:, 2:4])
            copy_pair("vm0", vm[:, 0])
            copy_pair("vm1", vm[:, 1])
            copy_pair("qd0", qd[:, 0:2])
            copy_pair("qd1", qd[:, 2:4])
            copy_pair("kd0", kd[:, 0:2])
            copy_pair("kd1", kd[:, 2:4])
            copy_pair("vd0", vd[:, 0])
            copy_pair("vd1", vd[:, 1])
            act.wait_ge(mod_ready, 4)
            nc.scalar.activation(small[:, 300:302], small[:, 298:300], ACT.Exp).then_inc(mod_ready, 1)

            def expo(s):
                act.wait_ge(s_max, s + 1)
                p, m, t = pbuf[s % 2], 304 + 4 * (s % 2), 312 + 4 * (s % 2)
                nc.scalar.activation(p[:, 0:128], p[:, 0:128], ACT.Exp, bias=small[:, m:m + 1], accum_out=small[:, t:t + 1])
                nc.scalar.activation(p[:, 128:384], p[:, 128:384], ACT.Exp, bias=small[:, m + 1:m + 2],
                                     accum_out=small[:, t + 1:t + 2]).then_inc(p_exp, 1)

            def pt_copy(u):
                act.wait_ge(t_done, u + 1)
                if u >= 2:
                    act.wait_ge(av_done, u - 1)
                nc.scalar.activation(ptb[u % 2], ps[:, 6, 0:384], ACT.Copy).then_inc(pt_evac, 1)

            def av_copy(u):
                act.wait_ge(av_done, u + 1)
                dst = qm[:, u // 2] if u < 8 else qd[:, u - 8]
                nc.scalar.activation(dst, ps[:, 7, 0:256], ACT.Copy).then_inc(av_evac, 1)

            def gate(name, dst):
                wait_tile(act, name)
                nc.scalar.activation(dst, bank(name), ACT.Sigmoid).then_inc(evac_sem(name), 1)

            expo(0)
            for u in range(12):
                if u + 1 < 8:
                    expo(u + 1)
                if u >= 8:
                    expo(2 * u - 8)
                    expo(2 * u - 7)
                pt_copy(u)
                if u < 8 and u % 2 == 1:
                    gate(f"gm{u // 2}", gm[:, u - 1:u + 1])
                if u >= 8:
                    gate(f"gd{u - 8}", gd[:, 2 * u - 16:2 * u - 14])
                if u >= 8 or u % 2 == 1:
                    av_copy(u)
            act.wait_ge(av_evac, 8)
            nc.scalar.activation(fm(0, 4), qd, ACT.Square).then_inc(osq_done, 1)
            act.wait_ge(oms_done, 1)
            nc.scalar.activation(fm(0, 4), fm(0, 4), ACT.Sqrt).then_inc(oroot_done, 1)

            norm_square(6)
            norm_root(6)
            norm_shift(6, 24)
            for c in range(TC):
                act.wait_ge(gmax_done, 1)
                ins = nc.scalar.activation(small[:, 100 + 4 * c:104 + 4 * c], small[:, 36 * c:36 * c + 4], ACT.Exp,
                                           bias=small[:, 96 + c:97 + c], accum_out=small[:, 110 + c:111 + c])
            ins.then_inc(gexp_done, 1)
            act.wait_ge(m2_ready, 1)
            nc.scalar.activation(small[:, 114:116], small[:, 112:114], ACT.Exp).then_inc(e2_done, 1)
            for q in range(4):
                act.wait_ge(htok_pe, q + 1)
                nc.scalar.activation(h2tok[:, q // 2, (q % 2) * 512:(q % 2 + 1) * 512], ps[:, q, :], ACT.Copy).then_inc(htok_ev, 1)
            for k in range(KC):
                act.wait_ge(gather_pe, k + 1)
                nc.scalar.activation(xs[:, k, 0:SLOTS], ps[:, k % 4, :], ACT.Copy).then_inc(gather_ev, 1)
            for q in range(2):
                act.wait_ge(combT_pe, q + 1)
                nc.scalar.activation(combT[:, 2 * q:2 * q + 2], ps[:, 4 + q, :], ACT.Copy).then_inc(combT_ev, 1)

            act.wait_ge(info_ready, 1)

            def expert(e):
                n_win = act.value_load(info[0:1, bass.ds(e + N_EXP, 1)], min_val=1, max_val=SEQ // WIN)
                first = act.value_load(info[0:1, bass.ds(e + 2 * N_EXP, 1)], min_val=0, max_val=N_EXP + SLOTS // WIN)
                with act.Fori(0, n_win) as w:
                    for h in range(2):
                        act.wait_ge(gu_done[h], first + w + 1 + h)
                        nc.scalar.activation(hidE[:, h * 256:(h + 1) * 256], ps[0:WIN, h, 0:256], ACT.Silu).then_inc(silu_done[h], 1)
                    act.wait_ge(down_done[0], first + w + 1)
                    nc.scalar.activation(yE[0], ps[0:WIN, 4, :], ACT.Copy).then_inc(y_ev[0], 1)
                act.wait_ge(gu_done[1], first + n_win + 1)
                act.sem_inc(gu_used, 1)

            with act.Fori(0, N_EXP) as e:
                expert(e)
            for q in range(0, 8, 2):
                act.wait_ge(yt_pe, q + 1)
                nc.scalar.activation(ystok[:, q // 2, 0:512], ps[:, q, :], ACT.Copy).then_inc(yt_act, 1)
            norm_square(7)
            norm_root(7)
            for q in range(4):
                act.wait_ge(fin_pe, q + 1)
                nc.scalar.activation(otok[:, q // 2, (q % 2) * 512:(q % 2 + 1) * 512], ps[:, q, :], ACT.Copy).then_inc(fin_ev, 1)

        @block.vector
        def _(dve):
            n_chain = [0]

            def link(ins):
                n_chain[0] += 1
                ins.then_inc(dve_ch, 1)
                dve.wait_ge(dve_ch, n_chain[0])

            def norm_scale(n, gains, last=None, dst=hT):
                dve.wait_ge(sum_done, n + 1)
                nc.vector.tensor_scalar(rstd[:], ps[:, 7, 0:SEQ], 1.0 / D, EPS, ALU.mult, ALU.add).then_inc(ms_done, 1)
                dve.wait_ge(root_done, n + 1)
                link(nc.vector.reciprocal(rstd[:], rstd[:]))
                for k in range(KC):
                    ins = nc.vector.scalar_tensor_tensor(out=dst[:, k], in0=xT[:, k], scalar=gains(k), in1=rstd[:], op0=ALU.mult, op1=ALU.mult)
                    if last is None:
                        ins.then_inc(h_part, 1)
                if last is not None:
                    ins.then_inc(last, 1)

            for q in range(4):
                dve.wait_ge(setup_pe, q + 1)
                ins = nc.vector.tensor_copy(xT[:, 2 * q:2 * q + 2], ps[:, q, :].rearrange("p (k t) -> p k t", k=2))
            ins.then_inc(x_ready, 1)
            dve.wait_ge(setup_pe, 5)
            nc.vector.tensor_copy(cols[:, 0:N_ROWS_A], ps[:, 4, 0:N_ROWS_A]).then_inc(setup_ev, 1)
            dve.wait_ge(setup_pe, 6)
            nc.vector.tensor_copy(cols[:, N_ROWS_A:], ps[:, 5, 0:N_ROWS_B]).then_inc(setup_ev, 1)
            dve.wait_ge(setup_ev, 2)
            nc.vector.memset(rec[:, :, 0:3], 0.0).then_inc(pad_zero, 1)
            norm_scale(0, lambda k: col(R_MIX + k), h_ready)

            dve.wait_ge(sp8_ready, 1)
            link(nc.vector.tensor_scalar(small[:, 280:288], cols[:, R_LAM:R_LAM + 8], -1.0, 0.0, ALU.mult, ALU.max))
            link(nc.vector.tensor_tensor(small[:, 280:288], small[:, 280:288], small[:, 272:280], ALU.add))
            link(nc.vector.tensor_scalar(small[:, 280:288], small[:, 280:288], 8.0, None, ALU.mult))
            nc.vector.tensor_scalar(small[:, 288:296], small[:, 280:288], -1.0, None, ALU.mult).then_inc(sp8_ready, 1)

            for hf in range(2):
                ms = range(HALF * hf, HALF * hf + HALF)
                wait_evac(dve, f"rec{2 * hf}")
                wait_evac(dve, f"rec{2 * hf + 1}")
                for m in ms:
                    ins = nc.vector.tensor_scalar(cv[:, m], rec[:, m, 3:3 + SEQ], col(R_CW + 24 + m), col(R_CB + m), ALU.mult, ALU.add)
                link(ins)
                for j in range(3):
                    for m in ms:
                        ins = nc.vector.scalar_tensor_tensor(out=cv[:, m], in0=rec[:, m, j:j + SEQ], scalar=col(R_CW + 8 * j + m),
                                                             in1=cv[:, m], op0=ALU.mult, op1=ALU.add)
                    if j < 2:
                        link(ins)
                ins.then_inc(conv_done, 1)
            for hf in range(2):
                hs = slice(HALF * hf, HALF * hf + HALF)
                wait_evac(dve, f"gate{2 * hf}_1")
                wait_evac(dve, f"gate{2 * hf + 1}_1")
                dve.wait_ge(conv_done, 2)
                link(nc.vector.tensor_tensor(ib[:, hs], ib[:, hs], cv[:, hs], ALU.mult))
                dve.wait_ge(tile_done, TILE_NO["gate3_1"] + 1)
                dve.wait_ge(ta_done, hf + 1)
                link(nc.vector.tensor_scalar(cv[:, hs], tb[:, hs], 1.0, None, ALU.add))
                link(nc.vector.reciprocal(cv[:, hs], cv[:, hs]))
                link(nc.vector.tensor_tensor(tb[:, hs], tb[:, hs], cv[:, hs], ALU.mult))
                nc.vector.tensor_scalar(tb[:, hs], tb[:, hs], 1e-30, None, ALU.max).then_inc(ratio_done, 1)
            for hf in range(2):
                hs = slice(HALF * hf, HALF * hf + HALF)
                dve.wait_ge(mult_done, hf + 1)
                link(nc.vector.tensor_tensor(ib[:, hs], ib[:, hs], tb[:, hs], ALU.mult))
                for m in range(HALF * hf, HALF * hf + HALF):
                    ins = nc.vector.tensor_tensor_scan(cv[:, m], hT[:, m], ib[:, m], 0.0, ALU.mult, ALU.add)
                link(ins)
                for m in range(HALF * hf, HALF * hf + HALF):
                    nc.vector.tensor_tensor(gl[:, m], gl[:, m], cv[:, m], ALU.mult).then_inc(y_done, 1)
            wait_used(dve, "lo1")
            for k in range(KC):
                ins = nc.vector.scalar_tensor_tensor(out=xT[:, k], in0=ps[:, 4 + k // 2, (k % 2) * 256:(k % 2 + 1) * 256], scalar=col(R_BOUT + k),
                                                     in1=xT[:, k], op0=ALU.add, op1=ALU.add)
            ins.then_inc(x_ready, 1)

            def add_residual(last):
                wait_used(dve, last)
                for b in range(4):
                    ins = nc.vector.tensor_tensor(xT[:, 2 * b:2 * b + 2], ps[:, 4 + b, :].rearrange("p (k t) -> p k t", k=2), xT[:, 2 * b:2 * b + 2], ALU.add)
                ins.then_inc(x_ready, 1)

            def ffn(layer):
                def gate_up(slot, step):
                    dve.wait_ge(ffn_silu, step + 1)
                    nc.vector.tensor_tensor(hid[:, slot], hid[:, slot], ps[:, 2 * slot + 1, :], ALU.mult).then_inc(ffn_hid, 1)

                base = layer * FFN_STEPS
                for s in range(3):
                    gate_up(s % 2, base + s)
                with dve.Fori(0, (FFN_STEPS - 3) // 2) as j:
                    gate_up(1, 2 * j + base + 3)
                    gate_up(0, 2 * j + base + 4)

            norm_scale(1, lambda k: col(R_FFN + k), h_ready)
            ffn(0)
            add_residual(f"ffn0_{FFN_STEPS - 1}")

            norm_scale(2, lambda k: col(R_MIX + KC + k), h_ready)
            dve.wait_ge(mod_ready, 1)
            for u in range(12):
                w = ring_b[:, (u % 6) * UNIT:(u % 6 + 1) * UNIT].rearrange("p (k f) -> p k f", k=KC)
                dve.wait_ge(ada_loaded[u % 6], 16 * (u // 6 + 1))
                acc = ada_acc[:, u % 2]
                if u >= 2:
                    dve.wait_ge(ada_psum, u - 1)
                link(nc.vector.tensor_scalar(acc, w[:, 0], small[:, 256:257], None, ALU.mult))
                for k in range(1, KC):
                    ins = nc.vector.scalar_tensor_tensor(out=acc, in0=w[:, k], scalar=small[:, 256 + k:257 + k], in1=acc, op0=ALU.mult, op1=ALU.add)
                    if k < KC - 1:
                        link(ins)
                ins.then_inc(ada_used, 1)
            dve.wait_ge(ada_psum, 12)
            link(nc.vector.tensor_tensor(ada[:], ps[:, 6, 0:48], cols[:, N_ROWS_A + R_ADA:N_ROWS_A + R_ADA + 48], ALU.add))
            link(nc.vector.scalar_tensor_tensor(out=gain[:, 0], in0=ada[:, 8:16], scalar=1.0, in1=cols[:, N_ROWS_A + R_N1:N_ROWS_A + R_N1 + 8],
                                                op0=ALU.add, op1=ALU.mult))
            nc.vector.scalar_tensor_tensor(out=gain[:, 1], in0=ada[:, 32:40], scalar=1.0, in1=cols[:, N_ROWS_A + R_N2:N_ROWS_A + R_N2 + 8],
                                           op0=ALU.add, op1=ALU.mult).then_inc(mod_ready, 1)

            def soft_mask(h):
                b = h % 2
                dve.wait_ge(soft_done, h + 1)
                if h >= 2:
                    dve.wait_ge(suf_done, h - 1)
                    dve.wait_ge(w_exp, h - 1)
                link(nc.vector.tensor_scalar(sk_p[b], ps[:, b, 0:384], SCALE, 0.0, ALU.mult, ALU.max))
                link(nc.vector.tensor_tensor(sk_p[b], sk_p[b], sk_e[b], ALU.add))
                link(nc.vector.scalar_tensor_tensor(out=sk_t[b], in0=ps[:, b, 0:384], scalar=SCALE, in1=sk_p[b], op0=ALU.mult, op1=ALU.subtract))
                nc.vector.tensor_tensor(sk_p[b], sk_p[b], stick, ALU.mult).then_inc(spm_done, 1)

            def argument(h):
                b = h % 2
                dve.wait_ge(suf_done, h + 1)
                nc.vector.tensor_tensor(sk_t[b], sk_t[b], ps[:, 2 + b, 0:384], ALU.subtract).then_inc(arg_done, 1)

            soft_mask(0)
            for h in range(HEADS):
                if h + 1 < HEADS:
                    soft_mask(h + 1)
                argument(h)
            add_residual("wo1")
            norm_scale(3, lambda k: col(R_FFN + KC + k), h_ready)
            ffn(1)
            add_residual(f"ffn1_{FFN_STEPS - 1}")

            norm_scale(4, lambda k: col(R_FIN1 + k), x_ready, xT)
            dve.wait_ge(mod_ready, 2)
            dve.wait_ge(lam_in, 16 * 6)
            for i in range(2):
                link(nc.vector.tensor_tensor(small[:, 2 * i * HD:(2 * i + 1) * HD], small[:, 2 * i * HD:(2 * i + 1) * HD],
                                             small[:, (2 * i + 1) * HD:(2 * i + 2) * HD], ALU.mult))
                ins = nc.vector.reduce_sum(small[:, 298 + i:299 + i], small[:, 2 * i * HD:(2 * i + 1) * HD], AX_X)
                ins.then_inc(mod_ready, 1)
            norm_scale(5, lambda k: gain[:, 0, k:k + 1])

            dve.wait_ge(rope_in, 16)
            for i, (nm, x) in enumerate((("qm", qm), ("km", km), ("qd", qd), ("kd", kd))):
                for d in range(2):
                    r = 2 * i + d
                    xx = x[:, 2 * d:2 * d + 2]
                    t3 = rope_t.rearrange("p (k t) -> p k t", k=2)
                    u3 = rope_u.rearrange("p (k t) -> p k t", k=2)
                    wait_tile(dve, f"rot{r}")
                    for kk in range(2):
                        nc.vector.tensor_tensor(t3[:, kk], xx[:, kk], rope[:, 0:256], ALU.mult)
                        ins = nc.vector.tensor_tensor(u3[:, kk], bank(f"rot{r}")[:, kk * 256:(kk + 1) * 256], rope[:, 256:512], ALU.mult)
                    ins.then_inc(evac_sem(f"rot{r}"), 1)
                    wait_evac(dve, f"rot{r}")
                    ins = nc.vector.tensor_tensor(xx, t3, u3, ALU.add)
                    ins.then_inc(roped, 1)
                    dve.wait_ge(roped, r + 1)
            dve.wait_ge(mod_ready, 5)
            link(nc.vector.tensor_tensor(small[:, 302:303], small[:, 300:301], small[:, 301:302], ALU.subtract))
            link(nc.vector.tensor_scalar(small[:, 302:303], small[:, 302:303], LAM_INIT, None, ALU.add))

            def masked_max(s):
                b = s % 2
                p, m = pbuf[b], 304 + 4 * b
                dve.wait_ge(s_done, s + 1)
                if 2 <= s < 10:
                    dve.wait_ge(t_done, s - 1)
                elif s >= 10:
                    dve.wait_ge(t_done, (s - 8) // 2 + 8)
                link(nc.vector.scalar_tensor_tensor(out=p, in0=ps[:, 4 + b, 0:384], scalar=SCALE, in1=negm, op0=ALU.mult, op1=ALU.add))
                nc.vector.reduce_max(small[:, m:m + 1], p[:, 0:128], AX_X)
                link(nc.vector.reduce_max(small[:, m + 1:m + 2], p[:, 128:384], AX_X))
                nc.vector.tensor_scalar(small[:, m:m + 2], small[:, m:m + 2], -1.0, None, ALU.mult).then_inc(s_max, 1)

            def norm_head(u):
                b = u % 2
                dve.wait_ge(p_exp, u + 1)
                r = 312 + 4 * b
                link(nc.vector.reciprocal(small[:, r + 2:r + 4], small[:, r:r + 2]))
                p = pbuf[b]
                nc.vector.tensor_scalar(p[:, 0:128], p[:, 0:128], small[:, r + 2:r + 3], None, ALU.mult)
                nc.vector.tensor_scalar(p[:, 128:384], p[:, 128:384], small[:, r + 3:r + 4], None, ALU.mult).then_inc(p_norm, 1)

            def norm_diff(u):
                dve.wait_ge(p_exp, 8 + 2 * (u - 8) + 2)
                nc.vector.reciprocal(small[:, 314:316], small[:, 312:314])
                link(nc.vector.reciprocal(small[:, 318:320], small[:, 316:318]))
                link(nc.vector.tensor_scalar(small[:, 318:320], small[:, 318:320], small[:, 302:303], None, ALU.mult))
                nc.vector.tensor_scalar(pbuf[1][:, 0:128], pbuf[1][:, 0:128], small[:, 318:319], None, ALU.mult)
                link(nc.vector.tensor_scalar(pbuf[1][:, 128:384], pbuf[1][:, 128:384], small[:, 319:320], None, ALU.mult))
                for q, (lo, hi) in enumerate(((0, 128), (128, 384))):
                    ins = nc.vector.scalar_tensor_tensor(out=pbuf[0][:, lo:hi], in0=pbuf[0][:, lo:hi], scalar=small[:, 314 + q:315 + q],
                                                         in1=pbuf[1][:, lo:hi], op0=ALU.mult, op1=ALU.subtract)
                ins.then_inc(p_norm, 1)

            masked_max(0)
            for u in range(12):
                if u + 1 < 8:
                    masked_max(u + 1)
                if u < 8:
                    norm_head(u)
                else:
                    masked_max(2 * u - 8)
                    masked_max(2 * u - 7)
                    norm_diff(u)
            dve.wait_ge(osum_done, 1)
            link(nc.vector.tensor_scalar(flat(0, 1024), ps[:, 4:6, :].rearrange("p b n -> p (b n)"), 1.0 / P, EPS, ALU.mult, ALU.add))
            nc.vector.nop().then_inc(oms_done, 1)
            dve.wait_ge(oroot_done, 1)
            link(nc.vector.reciprocal(flat(0, 1024), flat(0, 1024)))
            link(nc.vector.tensor_scalar(small[:, 303:304], col(R_SUB, 1), 1.0 - LAM_INIT, None, ALU.mult))
            nc.vector.scalar_tensor_tensor(out=flat(WORK + 3072, 1024), in0=flat(WORK + 3072, 1024), scalar=small[:, 303:304], in1=flat(0, 1024),
                                           op0=ALU.mult, op1=ALU.mult).then_inc(on_ready, 1)
            for i in range(4):
                wait_tile(dve, f"ym{i}")
                wait_evac(dve, f"gm{i}")
                g2 = gm[:, 2 * i:2 * i + 2]
                nc.vector.tensor_tensor(g2, bank(f"ym{i}").rearrange("p (k t) -> p k t", k=2), g2, ALU.mult).then_inc(evac_sem(f"ym{i}"), 1)
            for i in range(4):
                wait_tile(dve, f"yd{i}")
                wait_evac(dve, f"gd{i}")
                wait_evac(dve, f"ym{i}")
                g2 = gd[:, 2 * i:2 * i + 2]
                nc.vector.tensor_tensor(g2, bank(f"yd{i}").rearrange("p (k t) -> p k t", k=2), g2, ALU.mult).then_inc(evac_sem(f"yd{i}"), 1)
                wait_evac(dve, f"yd{i}")
                nc.vector.tensor_tensor(gm[:, 2 * i:2 * i + 2], gm[:, 2 * i:2 * i + 2], g2, ALU.add).then_inc(merged_ready, 1)

            def gated_residual(at, bank0):
                for k in range(KC):
                    ins = nc.vector.scalar_tensor_tensor(out=xT[:, k], in0=ps[:, bank0 + k // 2, (k % 2) * 256:(k % 2 + 1) * 256],
                                                         scalar=ada[:, at + k:at + k + 1], in1=xT[:, k], op0=ALU.mult, op1=ALU.add)
                ins.then_inc(x_ready, 1)

            wait_used(dve, "out1")
            gated_residual(16, 4)

            norm_scale(6, lambda k: gain[:, 1, k:k + 1])
            dve.wait_ge(logit_done, 1)

            def sm(lo, n=1):
                return small[:, lo:lo + n]

            def both(f):
                for c in range(TC):
                    ins = f(c)
                link(ins)

            V = nc.vector
            LG, OHG, EM, O1, O2 = 0, 80, 120, 160, 224
            both(lambda c: V.tensor_tensor(sm(LG + 36 * c, 36), ps[:, 4, 36 * c:36 * c + 36], bias36[:], ALU.add))
            both(lambda c: V.reduce_max(sm(94 + c), sm(LG + 36 * c, 4), AX_X))
            for c in range(TC):
                ins = V.tensor_scalar(sm(96 + c), sm(94 + c), -1.0, None, ALU.mult)
            ins.then_inc(gmax_done, 1)

            def first_max(src, n, top, dst, tmp):
                both(lambda c: V.tensor_scalar(sm(dst(c), n), sm(src(c), n), sm(top(c)), -64.0, ALU.is_equal, ALU.mult))
                both(lambda c: V.tensor_tensor(sm(dst(c), n), sm(dst(c), n), iota8[:, 0:n], ALU.add))
                both(lambda c: V.tensor_reduce(sm(tmp + c), sm(dst(c), n), AX_X, ALU.min))
                both(lambda c: V.tensor_scalar(sm(dst(c), n), sm(dst(c), n), sm(tmp + c), None, ALU.is_equal))

            first_max(lambda c: LG + 36 * c, 4, lambda c: 94 + c, lambda c: OHG + 4 * c, 116)
            both(lambda c: V.tensor_scalar(sm(EM + 8 * c, 8), sm(LG + 36 * c + 4, 8), sm(OHG + 4 * c), None, ALU.mult))
            for g in range(1, N_GRP):
                both(lambda c: V.scalar_tensor_tensor(out=sm(EM + 8 * c, 8), in0=sm(LG + 36 * c + 4 + 8 * g, 8), scalar=sm(OHG + 4 * c + g),
                                                      in1=sm(EM + 8 * c, 8), op0=ALU.mult, op1=ALU.add))
            both(lambda c: V.reduce_max(sm(118 + c), sm(EM + 8 * c, 8), AX_X))
            first_max(lambda c: EM + 8 * c, 8, lambda c: 118 + c, lambda c: 136 + 8 * c, 116)
            both(lambda c: V.scalar_tensor_tensor(out=sm(EM + 8 * c, 8), in0=sm(136 + 8 * c, 8), scalar=-3e38, in1=sm(EM + 8 * c, 8),
                                                  op0=ALU.mult, op1=ALU.add))
            both(lambda c: V.reduce_max(sm(152 + c), sm(EM + 8 * c, 8), AX_X))
            for c in range(TC):
                ins = V.tensor_tensor(sm(112 + c), sm(152 + c), sm(118 + c), ALU.subtract)
            ins.then_inc(m2_ready, 1)
            first_max(lambda c: EM + 8 * c, 8, lambda c: 152 + c, lambda c: EM + 8 * c, 116)
            dve.wait_ge(e2_done, 1)
            dve.wait_ge(gexp_done, 1)
            link(V.tensor_scalar(sm(154, 2), sm(114, 2), 1.0, None, ALU.add))
            link(V.tensor_tensor(sm(154, 2), sm(154, 2), sm(110, 2), ALU.mult))
            link(V.reciprocal(sm(154, 2), sm(154, 2)))
            link(V.tensor_tensor(sm(156, 2), sm(154, 2), sm(114, 2), ALU.mult))
            for g in range(N_GRP):
                for c in range(TC):
                    V.tensor_scalar(sm(O1 + 32 * c + 8 * g, 8), sm(136 + 8 * c, 8), sm(OHG + 4 * c + g), None, ALU.mult)
                    ins = V.tensor_scalar(sm(O2 + 32 * c + 8 * g, 8), sm(EM + 8 * c, 8), sm(OHG + 4 * c + g), None, ALU.mult)
            link(ins)
            V.tensor_tensor(sm(320, 64), sm(O1, 64), sm(O2, 64), ALU.add).then_inc(mask_ready, 1)
            dve.wait_ge(pos_done, 1)
            START = 0
            link(V.tensor_copy(sm(32, 32), ps[:, 5, 64:96]))
            link(V.tensor_tensor_scan(sm(START, 32), cst[:, C_ONES:C_ONES + 32], sm(32, 32), 0.0, ALU.mult, ALU.add))
            link(V.tensor_tensor(sm(START, 32), sm(START, 32), sm(32, 32), ALU.subtract))
            both(lambda c: V.tensor_tensor(sm(320 + 32 * c, 32), ps[:, 5, 32 * c:32 * c + 32], sm(START, 32), ALU.add))
            link(V.tensor_tensor(sm(O1, 64), sm(O1, 64), sm(320, 64), ALU.mult))
            link(V.tensor_tensor(sm(O2, 64), sm(O2, 64), sm(320, 64), ALU.mult))
            both(lambda c: V.reduce_sum(sm(384 + c), sm(O1 + 32 * c, 32), AX_X))
            both(lambda c: V.reduce_sum(sm(386 + c), sm(O2 + 32 * c, 32), AX_X))
            dve.wait_ge(slotno_in, 16)
            for c in range(TC):
                link(V.tensor_scalar(pick_t, slot_no, sm(384 + c), None, ALU.is_equal))
                link(V.scalar_tensor_tensor(out=pick[:, c], in0=slot_no, scalar=sm(386 + c), in1=pick_t, op0=ALU.is_equal, op1=ALU.add))
            V.nop().then_inc(pick_ready, 1)
            for c in range(TC):
                link(V.tensor_scalar(pick_t, slot_no, sm(384 + c), sm(154 + c), ALU.is_equal, ALU.mult))
                link(V.tensor_scalar(comb[:, c], slot_no, sm(386 + c), sm(156 + c), ALU.is_equal, ALU.mult))
                link(V.tensor_tensor(comb[:, c], comb[:, c], pick_t, ALU.add))
            V.nop().then_inc(comb_ready, 1)
            link(V.tensor_scalar(sm(96, 32), sm(32, 32), float(WIN), 1.0, ALU.is_gt, ALU.add))
            for w in range(2, SEQ // WIN):
                link(V.scalar_tensor_tensor(out=sm(96, 32), in0=sm(32, 32), scalar=float(w * WIN), in1=sm(96, 32), op0=ALU.is_gt, op1=ALU.add))
            link(V.tensor_tensor_scan(sm(128, 32), cst[:, C_ONES:C_ONES + 32], sm(96, 32), 0.0, ALU.mult, ALU.add))
            link(V.tensor_tensor(sm(128, 32), sm(128, 32), sm(96, 32), ALU.subtract))
            V.tensor_copy(info[:, 0:32], small[0:1, 0:32])
            V.tensor_copy(info[:, 32:64], small[0:1, 96:128])
            V.tensor_copy(info[:, 64:96], small[0:1, 128:160]).then_inc(info_ready, 1)
            dve.wait_ge(gather_pe, KC)
            link(V.memset(xs[:, :, SLOTS:], 0.0))
            V.nop().then_inc(gather_ev, 1)

            dve.wait_ge(info_ready, 1)
            dve.wait_ge(combT_ev, 2)
            V.nop().then_inc(win_evac, 1)

            def expert(e):
                start = dve.value_load(info[0:1, bass.ds(e, 1)], min_val=0, max_val=SLOTS)
                n_win = dve.value_load(info[0:1, bass.ds(e + N_EXP, 1)], min_val=1, max_val=SEQ // WIN)
                first = dve.value_load(info[0:1, bass.ds(e + 2 * N_EXP, 1)], min_val=0, max_val=N_EXP + SLOTS // WIN)
                with dve.Fori(0, n_win) as w:
                    for h in range(2):
                        dve.wait_ge(silu_done[h], first + w + 1)
                        half = hidE[:, h * 256:(h + 1) * 256]
                        V.tensor_tensor(half, half, ps[0:WIN, h, 256:512], ALU.mult).then_inc(hid_done[h], 1)
                        dve.wait_ge(hidT_pe[h], first + w + 1)
                        V.tensor_copy(hidT[:, 2 * h:2 * h + 2], ps[:, 2 + h, 0:2 * WIN].rearrange("p (k s) -> p k s", k=2)).then_inc(hidT_ev[h], 1)
                    dve.wait_ge(down_done[1], first + w + 1)
                    V.tensor_copy(yE[1], ps[0:WIN, 5, :]).then_inc(y_ev[1], 1)
                    dve.wait_ge(ywin_pe, first + w + 1)
                    V.tensor_copy(window(ys, start, w).rearrange("p (b k) s -> p b k s", b=2),
                                  ps[:, 6:8, 0:HALF * WIN].rearrange("p b (k s) -> p b k s", k=HALF)).then_inc(win_evac, 1)
                dve.wait_ge(win_evac, first + n_win + 1)
                dve.sem_inc(expert_used, 1)

            with dve.Fori(0, N_EXP) as e:
                expert(e)
            for q in range(1, 8, 2):
                dve.wait_ge(yt_pe, q + 1)
                V.tensor_copy(ystok[:, q // 2, 512:1024], ps[:, q, :]).then_inc(yt_dve, 1)
            dve.wait_ge(y2_done, 1)
            gated_residual(40, 0)
            norm_scale(7, lambda k: col(R_FIN + k, 1), h_ready)

        @block.tensor
        def _(pe):
            mm = nc.tensor.matmul

            def norm_sums(n):
                pe.wait_ge(sq_done, n + 1)
                for k in range(KC):
                    ins = mm(ps[:, 7, 0:SEQ], ones, hT[:, k], start=(k == 0), stop=(k == KC - 1))
                ins.then_inc(sum_done, 1)

            def start_tile(name):
                t = TILE_NO[name]
                if t >= 4:
                    pe.wait_ge(evac[t % 4], t // 4)
                return bank(name)

            def product_pair(name, w, m, kn, rhs):
                b = start_tile(name)
                for d in range(2):
                    for k in range(kn):
                        ins = mm(b[:, d * 256:(d + 1) * 256], w[:, k, (m + d) * P:(m + d + 1) * P], rhs[:, k], start=(k == 0), stop=(k == kn - 1))
                ins.then_inc(tile_done, 1)

            def token_major(name, w, x, c):
                b = start_tile(name)
                for k in range(KC):
                    ins = mm(b, x[:, k, c * P:(c + 1) * P], w[:, k], start=(k == 0), stop=(k == KC - 1))
                ins.then_inc(tile_done, 1)

            def accumulate(w, kn, k_first, rhs, first, last):
                for k in range(kn):
                    r = rhs(k_first + k)
                    for f in range(KC):
                        ins = mm(ps[:, 4 + f // 2, (f % 2) * 256:(f % 2 + 1) * 256], w[:, k, f * P:(f + 1) * P], r,
                                 start=(first and k == 0 and f % 2 == 0), stop=(last and k == kn - 1), skip_group_check=True)
                return ins

            pe.wait_ge(const_in, 16)
            pe.wait_ge(xtok_in, 16)
            for q in range(4):
                for d in range(2):
                    for c in range(TC):
                        ins = nc.tensor.transpose(ps[:, q, d * 256 + c * P:d * 256 + (c + 1) * P], xtok[:, c, (2 * q + d) * P:(2 * q + d + 1) * P], ident)
                ins.then_inc(setup_pe, 1)
            pe.wait_ge(rows_in, 16 * 15)
            nc.tensor.transpose(ps[:, 4, 0:N_ROWS_A], rows_a[0:N_ROWS_A, :], ident[0:N_ROWS_A, 0:N_ROWS_A]).then_inc(setup_pe, 1)
            nc.tensor.transpose(ps[:, 5, 0:N_ROWS_B], rows_b[0:N_ROWS_B, :], ident[0:N_ROWS_B, 0:N_ROWS_B]).then_inc(setup_pe, 1)

            norm_sums(0)
            pe.wait_ge(h_ready, 1)
            for nm in ("rec", "gb"):
                for u in range(2):
                    wait_unit(pe, f"{nm}{u}")
                    w = unit_view(f"{nm}{u}")
                    for h in range(2):
                        product_pair(f"{nm}{2 * u + h}", w, 2 * h, KC, hT)
            pe.wait_ge(gates_in, 16 * 8)
            w = unit_view("gates")
            for n in range(4):
                if n % 2 == 0:
                    pe.wait_ge(conv_done, n // 2 + 1)
                for g in range(2):
                    b = start_tile(f"gate{n}_{g}")
                    for d in range(2):
                        for c in range(2):
                            ins = mm(b[:, d * 256:(d + 1) * 256], w[:, g, n, c, d * P:(d + 1) * P], cv[:, 2 * n + c], start=(c == 0), stop=(c == 1))
                    ins.then_inc(tile_done, 1)
            for u in range(2):
                wait_unit(pe, f"lo{u}")
                for k in range(4):
                    pe.wait_ge(y_done, 4 * u + k + 1)
                    ins = accumulate(unit_view(f"lo{u}")[:, k:k + 1], 1, 4 * u + k, lambda k: gl[:, k], u == 0 and k == 0, u == 1 and k == 3)
                ins.then_inc(unit_summed, 1)

            def ffn(layer):
                base = layer * FFN_STEPS

                def gate_up(slot, step, loads):
                    wg, wu, _ = ffn_views(slot)
                    pe.wait_ge(fi_loaded[slot], 32 * loads)
                    for j, w in enumerate((wg, wu)):
                        for d in range(2):
                            for k in range(KC):
                                ins = mm(ps[:, 2 * slot + j, d * 256:(d + 1) * 256], w[:, k, d * P:(d + 1) * P], hT[:, k], start=(k == 0), stop=(k == KC - 1))
                    ins.then_inc(ffn_gu, 1)

                def down(slot, step, loads, first=False, last=False):
                    pe.wait_ge(fo_loaded[slot], 16 * loads)
                    pe.wait_ge(ffn_hid, step + 1)
                    ins = accumulate(ffn_views(slot)[2], 2, 0, lambda k: hid[:, slot, k * 256:(k + 1) * 256], first, last)
                    ins.then_inc(unit_summed, 1)

                l0 = 6 * layer
                l1 = 5 * layer
                gate_up(0, base, l0 + 1)
                gate_up(1, base + 1, l1 + 1)
                down(0, base, l0 + 1, first=True)
                with pe.Fori(0, (FFN_STEPS - 3) // 2) as j:
                    gate_up(0, 2 * j + base + 2, j + l0 + 2)
                    down(1, 2 * j + base + 1, j + l1 + 1)
                    gate_up(1, 2 * j + base + 3, j + l1 + 2)
                    down(0, 2 * j + base + 2, j + l0 + 2)
                gate_up(0, base + FFN_STEPS - 1, l0 + (FFN_STEPS - 3) // 2 + 2)
                down(1, base + FFN_STEPS - 2, l1 + (FFN_STEPS - 1) // 2)
                down(0, base + FFN_STEPS - 1, l0 + (FFN_STEPS + 1) // 2, last=True)

            norm_sums(1)
            pe.wait_ge(h_ready, 2)
            ffn(0)

            norm_sums(2)
            pe.wait_ge(h_ready, 3)

            def ada_sum(u):
                pe.wait_ge(ada_used, u + 1)
                for j in range(4):
                    ins = mm(ps[:, 6, 4 * u + j:4 * u + j + 1], ada_acc[:, u % 2, j * P:(j + 1) * P], ones[:, 0:1], start=True, stop=True)
                ins.then_inc(ada_psum, 1)

            n_ada = 0
            for nm in ("q", "k"):
                for u in range(2):
                    wait_unit(pe, f"{nm}{u}")
                    for h in range(2):
                        product_pair(f"{nm}{2 * u + h}", unit_view(f"{nm}{u}"), 2 * h, KC, hT)
                        ada_sum(n_ada)
                        n_ada += 1
            for u in range(2):
                wait_unit(pe, f"v{u}")
                for c in range(TC):
                    token_major(f"v{2 * u + c}", unit_view(f"v{u}"), hT, c)
                    ada_sum(n_ada)
                    n_ada += 1
            for t in range(4):
                wait_evac(pe, f"v{t}")

            def scores(h):
                lo = (h % 2) * HD
                if h >= 2:
                    pe.wait_ge(spm_done, h - 1)
                q, k, b = qT[lo:lo + HD, h // 2], kT[lo:lo + HD, h // 2], ps[:, h % 2]
                mm(b[:, 0:256], k[:, 0:P], q, start=True, stop=True)
                mm(b[:, 256:384], k[:, P:], q[:, P:], start=True, stop=True).then_inc(z_done, 1)

            def suffix(h):
                b = ps[:, 2 + h % 2]
                pe.wait_ge(spm_done, h + 1)
                if h >= 2:
                    pe.wait_ge(arg_done, h - 1)
                mm(b[:, 0:384], after, sk_p[h % 2], start=True, stop=False, skip_group_check=True)
                mm(b[:, 128:256], ones, sk_p[h % 2][:, 256:384], start=False, stop=True, skip_group_check=True).then_inc(suf_done, 1)

            def values(h):
                lo, c = (h % 2) * HD, h // 2
                b = ps[lo:lo + HD, 4 + c % 2]
                pe.wait_ge(w_done, h + 1)
                if h >= 4 and h % 2 == 0:
                    pe.wait_ge(o_evac, c - 1)
                mm(b[:, 0:256], vtok[:, 0, h * HD:(h + 1) * HD], sk_e[h % 2][:, 0:256], start=True, stop=False, skip_group_check=True)
                mm(b[:, 128:256], vtok[:, 1, h * HD:(h + 1) * HD], sk_e[h % 2][:, 256:384], start=False, stop=True, skip_group_check=True).then_inc(o_done, 1)

            scores(0)
            scores(1)
            for h in range(HEADS):
                suffix(h)
                if h >= 1:
                    values(h - 1)
                if h + 2 < HEADS:
                    scores(h + 2)
            values(HEADS - 1)
            pe.wait_ge(o_evac, 8)
            for u in range(2):
                wait_unit(pe, f"wo{u}")
                ins = accumulate(unit_view(f"wo{u}"), 4, 4 * u, lambda k: hT[:, k], u == 0, u == 1)
                ins.then_inc(unit_summed, 1)

            norm_sums(3)
            pe.wait_ge(h_ready, 4)
            ffn(1)

            norm_sums(4)
            norm_sums(5)
            pe.wait_ge(h_ready, 5)
            for nm in ("qm", "km", "vm", "qd", "kd", "vd"):
                wait_unit(pe, nm)
                for h in range(2):
                    if nm[0] == "v":
                        token_major(f"{nm}{h}", unit_view(nm), hT, h)
                    else:
                        product_pair(f"{nm}{h}", unit_view(nm), 2 * h, KC, hT)
            for i, (nm, x) in enumerate((("qm", qm), ("km", km), ("qd", qd), ("kd", kd))):
                for d in range(2):
                    wait_evac(pe, f"{nm}{d}")
                    b = start_tile(f"rot{2 * i + d}")
                    for kk in range(2):
                        ins = mm(b[:, kk * 256:(kk + 1) * 256], rot, x[:, 2 * d + kk], start=True, stop=True)
                    ins.then_inc(tile_done, 1)

            def softmax_scores(s):
                q, k = (qm, km) if s < 8 else (qd, kd)
                c, lo = (s % 8) // 2, (s % 2) * HD
                b = ps[:, 4 + s % 2]
                if s >= 2:
                    pe.wait_ge(s_max, s - 1)
                mm(b[:, 0:128], q[lo:lo + HD, c, 0:P], k[lo:lo + HD, c, 0:P], start=True, stop=True)
                mm(b[:, 128:384], q[lo:lo + HD, c, P:], k[lo:lo + HD, c, :], start=True, stop=True).then_inc(s_done, 1)

            def next_scores(u):
                if u < 8:
                    softmax_scores(u)
                elif u < 12:
                    softmax_scores(2 * u - 8)
                    softmax_scores(2 * u - 7)

            def gate_tile(nm, i):
                if i % 2 == 0:
                    wait_unit(pe, f"{nm}{i // 2}")
                product_pair(f"{nm}{i}", unit_view(f"{nm}{i // 2}"), 2 * (i % 2), KC, hT)

            pe.wait_ge(roped, 8)
            wait_evac(pe, "vm1")
            next_scores(0)
            for u in range(12):
                next_scores(u + 1)
                p = pbuf[u % 2] if u < 8 else pbuf[0]
                pe.wait_ge(p_norm, u + 1)
                if u >= 1:
                    pe.wait_ge(pt_evac, u)
                for i in range(3):
                    ins = nc.tensor.transpose(ps[:, 6, i * P:(i + 1) * P], p[:, i * P:(i + 1) * P], ident)
                ins.then_inc(t_done, 1)
                if u < 8 and u % 2 == 1:
                    gate_tile("gm", u // 2)
                if u >= 8:
                    gate_tile("gd", u - 8)
                pe.wait_ge(pt_evac, u + 1)
                pt = ptb[u % 2]
                if u < 8:
                    b = ps[(u % 2) * HD:(u % 2 + 1) * HD, 7]
                    v0, v1 = vm[:, 0, u * HD:(u + 1) * HD], vm[:, 1, u * HD:(u + 1) * HD]
                    if u % 2 == 0 and u:
                        pe.wait_ge(av_evac, u // 2)
                else:
                    b = ps[:, 7]
                    v0, v1 = vd[:, 0, (u - 8) * P:(u - 7) * P], vd[:, 1, (u - 8) * P:(u - 7) * P]
                    pe.wait_ge(av_evac, u - 4)
                mm(b[:, 0:256], v0, pt[:, 0:256], start=True, stop=False, skip_group_check=True)
                mm(b[:, 128:256], v1, pt[:, 256:384], start=False, stop=True, skip_group_check=True).then_inc(av_done, 1)
            pe.wait_ge(osq_done, 1)
            for i in range(4):
                ins = mm(ps[:, 4 + i // 2, (i % 2) * 256:(i % 2 + 1) * 256], ones, fm(0, 4)[:, i], start=True, stop=True)
            ins.then_inc(osum_done, 1)
            wait_unit(pe, "pm")
            for i in range(4):
                product_pair(f"ym{i}", unit_view("pm"), 2 * i, 4, qm)
            pe.wait_ge(on_ready, 1)
            wait_unit(pe, "pd")
            for i in range(4):
                product_pair(f"yd{i}", unit_view("pd"), 2 * i, 4, qd)
            for u in range(2):
                wait_unit(pe, f"out{u}")
                pe.wait_ge(merged_ready, 2 * u + 2)
                ins = accumulate(unit_view(f"out{u}"), 4, 4 * u, lambda k: gm[:, k], u == 0, u == 1)
                ins.then_inc(unit_summed, 1)

            norm_sums(6)
            pe.wait_ge(h_ready, 6)
            pe.wait_ge(route_in, 32)
            for c in range(TC):
                for k in range(KC):
                    ins = mm(ps[:, 4, 36 * c:36 * c + 36], hT[:, k, c * P:(c + 1) * P], w_route[:, k], start=(k == 0), stop=(k == KC - 1))
            ins.then_inc(logit_done, 1)
            for q in range(4):
                for j in range(4):
                    ins = nc.tensor.transpose(ps[:, q, j * P:(j + 1) * P], hT[:, 4 * (q % 2) + j, (q // 2) * P:(q // 2 + 1) * P], ident)
                ins.then_inc(htok_pe, 1)
            pe.wait_ge(mask_ready, 1)
            m0, m1 = small[:, 320:352], small[:, 352:384]
            mm(ps[:, 5, 0:32], before, m0, start=True, stop=True)
            mm(ps[:, 5, 32:64], ones, m0, start=True, stop=False)
            mm(ps[:, 5, 32:64], before, m1, start=False, stop=True)
            mm(ps[:, 5, 64:96], ones, m0, start=True, stop=False)
            mm(ps[:, 5, 64:96], ones, m1, start=False, stop=True).then_inc(pos_done, 1)
            pe.wait_ge(htok_ev, 4)
            pe.wait_ge(pick_ready, 1)
            pe.wait_ge(comb_ready, 1)
            for k in range(KC):
                if k >= 4:
                    pe.wait_ge(gather_ev, k - 3)
                for c in range(TC):
                    ins = mm(ps[:, k % 4, :], h2tok[:, c, k * P:(k + 1) * P], pick[:, c], start=(c == 0), stop=(c == TC - 1))
                ins.then_inc(gather_pe, 1)
            for q in range(2):
                for s in range(2):
                    for c in range(TC):
                        ins = nc.tensor.transpose(ps[:, 4 + q, s * 256 + c * P:s * 256 + (c + 1) * P],
                                                  comb[:, c, (2 * q + s) * P:(2 * q + s + 1) * P], ident)
                ins.then_inc(combT_pe, 1)
            pe.wait_ge(gather_ev, KC + 1)
            pe.wait_ge(combT_ev, 2)
            pe.wait_ge(info_ready, 1)

            def expert(e, e3, loads):
                wg, wu, wd = expert_place(e3)
                n_win = pe.value_load(info[0:1, bass.ds(e + N_EXP, 1)], min_val=1, max_val=SEQ // WIN)
                first = pe.value_load(info[0:1, bass.ds(e + 2 * N_EXP, 1)], min_val=0, max_val=N_EXP + SLOTS // WIN)
                with pe.Fori(0, n_win) as w:
                    pe.wait_ge(xw_ready, first + w + 1)
                    pe.wait_ge(gu_loaded[e3], 32 * loads)

                    def product(h, wt, j):
                        for k in range(KC):
                            ins = mm(ps[0:WIN, h, j * 256:(j + 1) * 256], xw[:, k], wt[:, k, h * 256:(h + 1) * 256], start=(k == 0), stop=(k == KC - 1))
                        return ins

                    def turn(dst, rows, waits):
                        if waits:
                            return mm(dst, rows, ident[0:WIN, 0:WIN], start=True, stop=True)
                        return nc.tensor.transpose(dst, rows, ident[0:WIN, 0:WIN])

                    def hidden_transposes(h):
                        pe.wait_ge(hid_done[h], first + w + 1)
                        for k in range(2):
                            ins = turn(ps[:, 2 + h, k * WIN:(k + 1) * WIN], hidE[:, (2 * h + k) * P:(2 * h + k + 1) * P], k == 0)
                        ins.then_inc(hidT_pe[h], 1)

                    def down(k, h):
                        return mm(ps[0:WIN, 4 + h, :], hidT[:, k], wd[:, k, h * 512:(h + 1) * 512], start=(k == 0), stop=(k == EC - 1), skip_group_check=True)

                    product(0, wg, 0)
                    product(0, wu, 1).then_inc(gu_done[0], 1)
                    product(1, wg, 0)
                    hidden_transposes(0)
                    product(1, wu, 1).then_inc(gu_done[1], 1)
                    pe.wait_ge(dn_loaded[e3], 16 * loads)
                    pe.wait_ge(hidT_ev[0], first + w + 1)
                    down(0, 0)
                    down(0, 1)
                    hidden_transposes(1)
                    down(1, 0)
                    down(1, 1)
                    pe.wait_ge(hidT_ev[1], first + w + 1)
                    for h in range(2):
                        down(2, h)
                        down(3, h).then_inc(down_done[h], 1)
                    pe.wait_ge(win_evac, first + w + 1)
                    for h in range(2):
                        pe.wait_ge(y_ev[h], first + w + 1)
                        for j in range(HALF):
                            ins = turn(ps[:, 6 + h, j * WIN:(j + 1) * WIN], yE[h][:, j * P:(j + 1) * P], j == 0)
                    ins.then_inc(ywin_pe, 1)

            nc.tensor.nop().then_inc(gu_done[1], 1)
            with pe.Fori(0, N_EXP // 3) as j:
                for s in range(3):
                    expert(3 * j + s, s, j + 1)
            for e in range(N_EXP // 3 * 3, N_EXP):
                expert(e, e % 3, e // 3 + 1)

            first = pe.value_load(info[0:1, 3 * N_EXP - 1:3 * N_EXP], min_val=N_EXP - 1, max_val=N_EXP + SLOTS // WIN)
            n_win = pe.value_load(info[0:1, 2 * N_EXP - 1:2 * N_EXP], min_val=1, max_val=SEQ // WIN)
            pe.wait_ge(win_evac, first + n_win + 1)
            for q in range(8):
                for j in range(4):
                    ins = nc.tensor.transpose(ps[:, q, j * P:(j + 1) * P], ys[:, 4 * (q % 2) + j, (q // 2) * P:(q // 2 + 1) * P], ident)
                ins.then_inc(yt_pe, 1)
            pe.wait_ge(yt_act, 4)
            pe.wait_ge(yt_dve, 4)
            for f in range(KC):
                for s in range(SC):
                    ins = mm(ps[:, f // 2, (f % 2) * 256:(f % 2 + 1) * 256], ystok[:, s, f * P:(f + 1) * P], combT[:, s], start=(s == 0), stop=(s == SC - 1))
            ins.then_inc(y2_done, 1)
            norm_sums(7)
            pe.wait_ge(h_ready, 7)
            for q in range(4):
                for j in range(4):
                    ins = nc.tensor.transpose(ps[:, q, j * P:(j + 1) * P], hT[:, 4 * (q % 2) + j, (q // 2) * P:(q // 2 + 1) * P], ident)
                ins.then_inc(fin_pe, 1)


def constant_arrays():
    i = np.arange(P)
    table = np.zeros((P, N_CONST), np.float32)
    table[:, C_ID:C_ID + P] = np.eye(P)
    table[:, C_AFTER:C_AFTER + P] = i[:, None] > i[None, :]
    table[:, C_BEFORE:C_BEFORE + P] = i[:, None] < i[None, :]
    table[:, C_ONES:C_ONES + P] = 1.0
    half = HD // 2
    for o in range(P):
        if o % HD < half:
            table[o + half, C_ROT + o] = -1.0
        else:
            table[o - half, C_ROT + o] = 1.0
    strict = (i[:, None] < i[None, :]).astype(np.float32)
    table[:, C_STICK:C_STICK + 384] = np.concatenate([strict, np.ones((P, P)), strict], axis=1)
    causal = np.where(i[None, :] <= i[:, None], 0.0, NEG)
    table[:, C_NEG:C_NEG + 384] = np.concatenate([causal, np.zeros((P, P)), causal], axis=1)
    table[:, C_IOTA:] = np.arange(GRP)
    inv = (1.0 / (np.float32(10000.0) ** (np.arange(0, HD, 2, dtype=np.float32) / np.float32(HD)))).astype(np.float32)
    ang = (inv[:, None] * np.arange(SEQ, dtype=np.float32)[None, :]).astype(np.float32)
    ang = ang[i % half]
    rope = np.concatenate([np.cos(ang), np.sin(ang)], axis=1).astype(np.float32)
    slots = np.broadcast_to(np.arange(SLOTS, dtype=np.float32), (P, SLOTS)).copy()
    return {"constants": table, "rope": rope, "slot_numbers": slots}


_INS = ["x", "mix_norm", "ffn_norm", "final_norm", "lru_w_in", "lru_b_in", "lru_conv_w", "lru_conv_b", "lru_gate_w", "lru_gate_b",
        "lru_lambda", "lru_w_out", "lru_b_out", "attn_w_qkv", "attn_w_o", "ffn_w_in", "ffn_w_out", "c_2", "w_ada_2", "b_ada_2",
        "norm1_g_2", "w_in_2", "lambda_q1_2", "lambda_k1_2", "lambda_q2_2", "lambda_k2_2", "diff_subln_g_2", "w_proj_moba_2",
        "w_proj_diff_2", "w_out_2", "norm2_g_2", "w_group_2", "b_group_2", "w_expert_2", "b_expert_2", "w_gate_2", "w_up_2",
        "w_down_2", "final_g_2"]


def kernel(**inputs):
    import concourse.bacc as _bacc
    from concourse.bass_utils import run_bass_kernel_spmd as _run

    nc = _bacc.Bacc("TRN2", target_bir_lowering=False, num_devices=1)
    arrays, aps = {}, {}
    given = {name: np.ascontiguousarray(inputs[name]) for name in _INS}
    for name, array in {**given, **constant_arrays()}.items():
        arrays[f"in_{name}"] = array
        aps[name] = nc.dram_tensor(f"in_{name}", array.shape, mybir.dt.from_np(array.dtype), kind="ExternalInput").ap()
    out = nc.dram_tensor("out", (1, SEQ, D), F32, kind="ExternalOutput").ap()
    program(nc, aps, out)
    result = _run(nc, [arrays], core_ids=[0])
    return result.results[0]["out"]
```

```python
from contextlib import ExitStack

import numpy as np

import concourse.bass as bass
from concourse import mybir

F32 = mybir.dt.float32
F32R = mybir.dt.float32r
I32 = mybir.dt.int32
ALU = mybir.AluOpType
ACT = mybir.ActivationFunctionType
AX_X = mybir.AxisListType.X

P = 128
SEQ = 256
D = 1024
KC = D // P
TC = SEQ // P
D_FF = 2816
FFN_COLS = 256
FFN_STEPS = D_FF // FFN_COLS
HEADS = 16
HD = 64
N_EXP, N_GRP, GRP = 32, 4, 8
D_EXP = 512
EC = D_EXP // P
SLOTS = 2 * SEQ
SC = SLOTS // P
WIN = 64
SLOT_PAD = SLOTS + WIN
EPS = 1e-6
SCALE = HD ** -0.5
NEG = -1e30
LAM_INIT = 0.2
HALF = KC // 2

C_ID, C_AFTER, C_BEFORE, C_ONES, C_ROT, C_STICK, C_NEG = 0, 128, 256, 384, 512, 640, 1024
C_IOTA = 1408
N_CONST = C_IOTA + GRP

R_MIX, R_FFN, R_BIN, R_CW, R_CB, R_GB, R_LAM, R_BOUT, R_FIN1, N_ROWS_A = 0, 16, 32, 48, 80, 88, 104, 112, 120, 128
R_N1, R_N2, R_FIN, R_ADA, R_SUB, R_C, N_ROWS_B = 0, 8, 16, 24, 72, 73, 81

UNITS = ([f"rec{i}" for i in range(2)] + [f"gb{i}" for i in range(2)] + ["gates"] + [f"lo{i}" for i in range(2)]
         + [f"ffn0_{i}" for i in range(FFN_STEPS)]
         + ["q0", "q1", "k0", "k1", "v0", "v1", "wo0", "wo1"]
         + [f"ffn1_{i}" for i in range(FFN_STEPS)]
         + ["qm", "km", "vm", "qd", "kd", "vd", "gm0", "gm1", "gd0", "gd1", "pm", "pd", "out0", "out1"])
UNIT = 4096
FFN_UNIT = 6144
RING_A = 3 * UNIT
MATRIX = 4096
SUM_BANK = (7, 0, 0, 0, 0, 0, 0, 4)
PART_PAIRS = ((0, 0), (1, 0), (0, 1))
UNIT_NO = {n: i for i, n in enumerate(UNITS)}

TILES = ([f"rec{i}" for i in range(4)] + [f"gb{i}" for i in range(4)] + [f"gate{n}_{g}" for n in range(4) for g in range(2)]
         + [f"q{i}" for i in range(4)] + [f"k{i}" for i in range(4)] + [f"v{i}" for i in range(4)]
         + ["qm0", "qm1", "km0", "km1", "vm0", "vm1", "qd0", "qd1", "kd0", "kd1", "vd0", "vd1"]
         + [f"rot{i}" for i in range(8)]
         + [f"gm{i}" for i in range(4)] + [f"gd{i}" for i in range(4)]
         + [f"ym{i}" for i in range(4)] + [f"yd{i}" for i in range(4)])
TILE_NO = {n: i for i, n in enumerate(TILES)}

SUMMED = [n for n in UNITS if n[:2] in ("lo", "wo") or n[:3] in ("ffn", "out")]
LAST_TILE = {"rec0": "rec1", "rec1": "rec3", "gb0": "gb1", "gb1": "gb3", "gates": "gate3_1", "q0": "q1", "q1": "q3", "k0": "k1",
             "k1": "k3", "v0": "v1", "v1": "v3", "qm": "qm1", "km": "km1", "vm": "vm1", "qd": "qd1", "kd": "kd1", "vd": "vd1",
             "gm0": "gm1", "gm1": "gm3", "gd0": "gd1", "gd1": "gd3", "pm": "ym3", "pd": "yd3"}


def summed_by(name):
    return SUMMED.index(name) + 1


def ring_places():
    places, at, previous = [], 0, None
    for name in UNITS:
        size = FFN_UNIT if name.startswith("ffn") else UNIT
        if size != previous or at + size > RING_A:
            at = 0
        places.append((at, size))
        at, previous = at + size, size
    before = []
    for n, (a, s) in enumerate(places):
        clash = [m for m in range(n) if places[m][0] < a + s and a < places[m][0] + places[m][1]]
        before.append(UNITS[max(clash)] if clash else None)
    return places, before


def program(nc, a, ys, out):
    places, unit_before = ring_places()
    with ExitStack() as ctx:
        def sb(name, shape, dt=F32):
            return ctx.enter_context(nc.sbuf_tensor(name, shape, dt))

        def sem(name):
            return ctx.enter_context(nc.semaphore(name))

        ring_a = sb("ring_a", [P, RING_A])
        ring_b = sb("ring_b", [P, 2 * MATRIX])
        parts = sb("parts", [P, 4 * MATRIX], F32R)
        xT = sb("xT", [P, KC, SEQ])
        with nc.sbuf_tensor("big_parts", [P, 2048 + 9728], F32R) as big_parts:
            pass
        big = sb("big", [P, 2048 + 9728])
        cst = sb("cst", [P, N_CONST])
        cols = sb("cols", [P, N_ROWS_A + N_ROWS_B])
        rstd = sb("rstd", [P, SEQ])
        ada = sb("ada", [P, 48])
        gain = sb("gain", [P, 2, KC])
        small = sb("small", [P, 400])
        bias36 = sb("bias36", [P, N_GRP + N_EXP])
        info = sb("info", [1, 3 * N_EXP], I32)
        ps = ctx.enter_context(nc.psum_tensor("ps", [P, 8, 512], F32))

        ident = cst[:, C_ID:C_ID + P]
        after = cst[:, C_AFTER:C_AFTER + P]
        before = cst[:, C_BEFORE:C_BEFORE + P]
        ones = cst[:, C_ONES:C_ONES + P]
        rot = cst[:, C_ROT:C_ROT + P]
        stick = cst[:, C_STICK:C_STICK + 384]
        negm = cst[:, C_NEG:C_NEG + 384]
        iota8 = cst[:, C_IOTA:C_IOTA + GRP]

        def flat(lo, n):
            return big[:, lo:lo + n]

        def fm(lo, k=KC):
            return flat(lo, k * SEQ).rearrange("p (k t) -> p k t", k=k)

        hT = fm(0)
        WORK = 2048
        rec = flat(WORK, KC * (SEQ + 3)).rearrange("p (k t) -> p k t", k=KC)
        tb = fm(WORK)
        cv = fm(WORK + 2080)
        gl = fm(WORK + 2080 + 2048)
        ib = fm(WORK + 2080 + 4096)
        xtok = flat(WORK + 2080 + 4096, 2048).rearrange("p (c f) -> p c f", c=TC)
        rows_a = flat(WORK, P)
        rows_b = flat(WORK + P, P)
        qT, kT = fm(WORK), fm(WORK + 2048)
        vtok = flat(WORK + 4096, 2048).rearrange("p (c f) -> p c f", c=TC)
        sk = flat(WORK + 6144, 6 * 512).rearrange("p (b n) -> p b n", b=6)
        sk_e, sk_p, sk_t = ([sk[:, 2 * i + b, 0:384] for b in range(2)] for i in range(3))
        hid = flat(WORK, 2 * 512).rearrange("p (b n) -> p b n", b=2)
        h_part_of = [big_parts[:, WORK + 1024 + i * 2048:WORK + 3072 + i * 2048].rearrange("p (k t) -> p k t", k=KC) for i in range(2)]
        hid_part = [[big_parts[:, WORK + 5120 + (2 * b + i) * 512:WORK + 5632 + (2 * b + i) * 512] for i in range(2)] for b in range(2)]
        qm, km = fm(WORK, 4), fm(WORK + 1024, 4)
        vm = flat(WORK + 2048, 1024).rearrange("p (c f) -> p c f", c=TC)
        gd = fm(WORK + 1024)
        qd, kd = fm(WORK + 3072, 4), fm(WORK + 4096, 4)
        vd = flat(WORK + 5120, 1024).rearrange("p (c f) -> p c f", c=TC)
        gm = fm(WORK + 6144)
        TMP = WORK + 8192
        rope = flat(TMP, 512)
        rope_t = flat(TMP + 512, 512)
        rope_u = flat(TMP + 1024, 512)
        ada_acc = flat(WORK + 6144, 1024).rearrange("p (b n) -> p b n", b=2)
        pbuf = [flat(TMP + 384 * i, 384) for i in range(2)]
        ptb = [flat(TMP + 768 + 384 * i, 384) for i in range(2)]
        h2tok = flat(2048, 2048).rearrange("p (c f) -> p c f", c=TC)
        pick = flat(4096, 1024).rearrange("p (c s) -> p c s", c=TC)
        slot_no = flat(5120, SLOTS)
        pick_t = flat(5632, SLOTS)
        xs = flat(5120, KC * SLOT_PAD).rearrange("p (k s) -> p k s", k=KC)
        combT = flat(9728, SC * SEQ).rearrange("p (s t) -> p s t", s=SC)
        comb = flat(10752, 1024).rearrange("p (c s) -> p c s", c=TC)
        xw = ring_a[:, 2 * UNIT:2 * UNIT + KC * WIN].rearrange("p (k s) -> p k s", k=KC)
        hidE = ring_a[0:WIN, 2 * UNIT + 512:2 * UNIT + 1024]
        yE = ring_a[0:WIN, 2 * UNIT + 1024:2 * UNIT + 2048]
        hidT = [big_parts[:, KC * SLOT_PAD + i * EC * WIN:KC * SLOT_PAD + (i + 1) * EC * WIN].rearrange("p (k s) -> p k s", k=EC) for i in range(2)]
        xp = [big_parts[:, 10752 + i * KC * WIN:10752 + (i + 1) * KC * WIN].rearrange("p (k s) -> p k s", k=KC) for i in range(2)]
        ystok = flat(5120, SC * D).rearrange("p (s f) -> p s f", s=SC)
        otok = flat(2048, 2048).rearrange("p (c f) -> p c f", c=TC)
        w_route = flat(WORK + 9728 - KC * 36, KC * 36).rearrange("p (k n) -> p k n", k=KC)

        def col(row, table=0):
            i = row + (N_ROWS_A if table else 0)
            return cols[:, i:i + 1]

        a_loaded = [sem(f"a_loaded{i}") for i in range(3)]
        fi_loaded = [sem(f"fi_loaded{i}") for i in range(2)]
        fo_loaded = [sem(f"fo_loaded{i}") for i in range(2)]
        unit_summed = sem("unit_summed")
        ada_loaded = [sem(f"ada_loaded{i}") for i in range(2)]
        ada_used = sem("ada_used")
        ada_psum = sem("ada_psum")
        gates_in = sem("gates_in")
        const_in, rows_in, xtok_in, rope_in, route_in = (sem(n) for n in ("const_in", "rows_in", "xtok_in", "rope_in", "route_in"))
        slotno_in = sem("slotno_in")
        lam_in = sem("lam_in")
        tile_done = sem("tile_done")
        evac = [sem(f"evac{b}") for b in range(4)]
        setup_pe, setup_ev = sem("setup_pe"), sem("setup_ev")
        x_ready = sem("x_ready")
        sq_done, sum_done, ms_done, root_done = (sem(n) for n in ("sq_done", "sum_done", "ms_done", "root_done"))
        h_part, h_ready = sem("h_part"), sem("h_ready")
        dve_ch, act_ch = sem("dve_ch"), sem("act_ch")
        pad_zero = sem("pad_zero")
        sp8_ready = sem("sp8_ready")
        conv_done, gate_sum, ta_done, ratio_done, mult_done, y_done = (
            sem(n) for n in ("conv_done", "gate_sum", "ta_done", "ratio_done", "mult_done", "y_done"))
        ffn_g, ffn_gu, ffn_silu, ffn_hid, ffn_hid_hi, ffn_hid_lo = (
            sem(n) for n in ("ffn_g", "ffn_gu", "ffn_silu", "ffn_hid", "ffn_hid_hi", "ffn_hid_lo"))
        fh_hi, fh_lo, fg_hi, fg_lo, fu_hi, fu_lo, fd_hi, fd_lo = (
            sem(n) for n in ("fh_hi", "fh_lo", "fg_hi", "fg_lo", "fu_hi", "fu_lo", "fd_hi", "fd_lo"))
        z_done, soft_done, spm_done, z_read, suf_done, arg_done, w_exp, w_done, o_done, o_evac = (
            sem(n) for n in ("z_done", "soft_done", "spm_done", "z_read", "suf_done", "arg_done", "w_exp", "w_done", "o_done", "o_evac"))
        mod_ready = sem("mod_ready")
        roped = sem("roped")
        s_done, s_max, p_exp, p_norm, t_done, pt_evac, av_done, av_evac = (
            sem(n) for n in ("s_done", "s_max", "p_exp", "p_norm", "t_done", "pt_evac", "av_done", "av_evac"))
        osq_done, osum_done, oms_done, oroot_done, on_ready = (
            sem(n) for n in ("osq_done", "osum_done", "oms_done", "oroot_done", "on_ready"))
        merged_ready = sem("merged_ready")
        logit_done, gexp_done, gmax_done, e2_done, m2_ready, mask_ready, pos_done = (
            sem(n) for n in ("logit_done", "gexp_done", "gmax_done", "e2_done", "m2_ready", "mask_ready", "pos_done"))
        htok_pe, htok_ev, pick_ready, comb_ready, gather_pe, gather_ev, combT_pe, combT_ev = (
            sem(n) for n in ("htok_pe", "htok_ev", "pick_ready", "comb_ready", "gather_pe", "gather_ev", "combT_pe", "combT_ev"))
        info_ready = sem("info_ready")
        g_loaded = [sem(f"g_loaded{i}") for i in range(2)]
        u_loaded, d_loaded = sem("u_loaded"), sem("d_loaded")
        g_used = sem("g_used")
        u_hi, u_lo, d_hi, d_lo = ([sem(f"{n}{h}") for h in range(2)] for n in ("u_hi", "u_lo", "d_hi", "d_lo"))

        def steps(name):
            return [sem(f"{name}_first"), sem(f"{name}_more")]

        def half_steps(name):
            return [[sem(f"{name}{h}_{q}") for h in range(2)] for q in ("first", "more")]

        xw_ready, xp_ready, gate_done, silu_done, y_stored = (steps(n) for n in ("xw_ready", "xp_ready", "gate_done", "silu_done", "y_stored"))
        up_done, hid_done, hidT_pe, hidT_hi, hidT_lo, down_done, y_ev = (
            half_steps(n) for n in ("up_done", "hid_done", "hidT_pe", "hidT_hi", "hidT_lo", "down_done", "y_ev"))
        ystok_in = sem("ystok_in")
        y2_done, fin_pe, fin_ev, stored = (sem(n) for n in ("y2_done", "fin_pe", "fin_ev", "stored"))

        def unit_view(name):
            at, _ = places[UNIT_NO[name]]
            v = ring_a[:, at:at + UNIT]
            if name == "gates":
                return v.rearrange("p (g n c d) -> p g n c d", g=2, n=4, c=2)
            if name[:2] in ("lo", "wo", "pm", "pd") or name[:3] == "out":
                return v.rearrange("p (k f) -> p k f", k=4)
            return v.rearrange("p (k f) -> p k f", k=KC)

        def ffn_views(slot):
            v = ring_a[:, slot * FFN_UNIT:(slot + 1) * FFN_UNIT]
            return (v[:, 0:2048].rearrange("p (k f) -> p k f", k=KC), v[:, 2048:4096].rearrange("p (k f) -> p k f", k=KC),
                    v[:, 4096:6144].rearrange("p (k f) -> p k f", k=2))

        def ffn_part(i, k):
            return [parts[:, (2 * i + q) * 2048:(2 * i + q + 1) * 2048].rearrange("p (k f) -> p k f", k=k) for q in range(2)]

        fg_part, fu_part, fd_part = ffn_part(0, KC), ffn_part(1, KC), ffn_part(2, 2)

        def ffn_loads(layer, n):
            return (6, 5)[n % 2] * layer + n // 2 + 1

        def unit_source(name):
            def columns(w, c):
                return w[:, c * 512:(c + 1) * 512].rearrange("(k p) n -> p k n", p=P)

            def krows(w, c):
                return w[c * 512:(c + 1) * 512, :].rearrange("(k p) n -> p k n", p=P)

            i = int(name[-1]) if name[-1].isdigit() else 0
            if name.startswith("rec"):
                return columns(a["lru_w_in"][0], 2 + i)
            if name.startswith("gb"):
                return columns(a["lru_w_in"][0], i)
            if name.startswith("lo"):
                return krows(a["lru_w_out"][0], i)
            if name.startswith("wo"):
                return krows(a["attn_w_o"][0], i)
            if name.startswith("out"):
                return krows(a["w_out_2"][0], i)
            if name == "pm":
                return krows(a["w_proj_moba_2"][0], 0)
            if name == "pd":
                return krows(a["w_proj_diff_2"][0], 0)
            if name in ("q0", "q1", "k0", "k1", "v0", "v1"):
                return columns(a["attn_w_qkv"][0], 2 * "qkv".index(name[0]) + i)
            return columns(a["w_in_2"][0], ["qm", "km", "vm", "qd", "kd", "vd", "gm0", "gm1", "gd0", "gd1"].index(name))

        load_count = {}
        for name in UNITS:
            if not name.startswith("ffn"):
                s = places[UNIT_NO[name]][0] // UNIT
                load_count[name] = (s, 1 + sum(1 for m in load_count if load_count[m][0] == s and m != "gates"))

        def wait_unit(eng, name):
            s, n = load_count[name]
            eng.wait_ge(a_loaded[s], 16 * n)

        def wait_used(eng, name):
            if name in SUMMED:
                eng.wait_ge(unit_summed, summed_by(name))
            else:
                eng.wait_ge(tile_done, TILE_NO[LAST_TILE[name]] + 1)

        def wait_tile(eng, name):
            eng.wait_ge(tile_done, TILE_NO[name] + 1)

        def wait_evac(eng, name):
            t = TILE_NO[name]
            eng.wait_ge(evac[t % 4], t // 4 + 1)

        def bank(name):
            return ps[:, TILE_NO[name] % 4, :]

        def evac_sem(name):
            return evac[TILE_NO[name] % 4]

        def kf(v, k):
            return v.rearrange("p (k f) -> p k f", k=k)

        g_place = [kf(ring_b[:, i * MATRIX:(i + 1) * MATRIX], KC) for i in range(2)]
        u_place, d_place = kf(ring_a[:, 0:MATRIX], KC), kf(ring_a[:, MATRIX:2 * MATRIX], EC)
        u_part = [kf(parts[:, i * MATRIX:(i + 1) * MATRIX], KC) for i in range(2)]
        d_part = [kf(parts[:, (2 + i) * MATRIX:(3 + i) * MATRIX], EC) for i in range(2)]

        def window(start, w):
            at = nc.s_assert_within(start + w * WIN, 0, SLOTS, skip_runtime_bounds_check_because="w * WIN is less than the expert's slots, which end by SLOTS, or w is 0")
            return bass.ds(at, WIN)

        def start_of(eng, e):
            return eng.value_load(info[0:1, bass.ds(e, 1)], min_val=0, max_val=SLOTS)

        def more_windows(eng, e):
            return (eng.value_load(info[0:1, bass.ds(e + N_EXP, 1)], min_val=0, max_val=SEQ // WIN - 1),
                    eng.value_load(info[0:1, bass.ds(e + 2 * N_EXP, 1)], min_val=0, max_val=SLOTS // WIN))

        def load_matrix(eng, dst, w, e, done):
            eng.dma_start(dst, a[w][0, bass.ds(e, 1)].rearrange("e (k p) f -> p (e k) f", p=P)).then_inc(done, 16)

        block = ctx.enter_context(nc.Block())

        @block.sync
        def _(sp):
            sp.dma_start(xtok, a["x"][0].rearrange("(c p) f -> p c f", p=P)).then_inc(xtok_in, 16)

            def load_unit(name):
                n = UNIT_NO[name]
                if unit_before[n]:
                    wait_used(sp, unit_before[n])
                s, _ = load_count[name]
                dst = unit_view(name)
                if name == "gates":
                    for g in range(2):
                        for b in range(4):
                            ins = sp.dma_start(dst[:, g, b], a["lru_gate_w"][0, g, b].rearrange("(c p) d -> p c d", p=P))
                            ins.then_inc(gates_in, 16)
                    return
                sp.dma_start(dst, unit_source(name)).then_inc(a_loaded[s], 16)

            def load_ffn(layer, i, slot, free=None):
                g, u, dn = ffn_views(slot)
                if free is not None:
                    sp.wait_ge(fu_lo, free)
                w_in, w_out = a["ffn_w_in"][layer], a["ffn_w_out"][layer]
                sp.dma_start(g, w_in[:, bass.ds(i * FFN_COLS, FFN_COLS)].rearrange("(k p) n -> p k n", p=P)).then_inc(fi_loaded[slot], 16)
                sp.dma_start(u, w_in[:, bass.ds(i * FFN_COLS + D_FF, FFN_COLS)].rearrange("(k p) n -> p k n", p=P)).then_inc(fi_loaded[slot], 16)
                if free is not None:
                    sp.wait_ge(fd_lo, free)
                sp.dma_start(dn, w_out[bass.ds(i * FFN_COLS, FFN_COLS), :].rearrange("(k p) n -> p k n", p=P)).then_inc(fo_loaded[slot], 16)

            def load_ffn_layer(layer):
                for i in range(2):
                    wait_used(sp, unit_before[UNIT_NO[f"ffn{layer}_{i}"]])
                    load_ffn(layer, i, i)
                gu = layer * FFN_STEPS + 1
                with sp.Fori(0, (FFN_STEPS - 3) // 2) as j:
                    for i in range(2):
                        load_ffn(layer, 2 * j + 2 + i, i, 2 * j + gu + i)
                load_ffn(layer, FFN_STEPS - 1, 0, gu + FFN_STEPS - 3)

            for name in UNITS:
                if name.startswith("ffn"):
                    if name.endswith("_0"):
                        load_ffn_layer(int(name[3]))
                    continue
                load_unit(name)
                if name in ("wo1", "qm"):
                    sp.wait_ge(ada_used, 12)
                    load_matrix(sp, g_place[name == "qm"], "w_gate_2", int(name == "qm"), g_loaded[name == "qm"])
                if name == "kd":
                    sp.wait_ge(h_ready, 4 * KC)
                    sp.dma_start(rope, a["rope"]).then_inc(rope_in, 16)
            wait_used(sp, "out1")
            load_matrix(sp, u_place, "w_up_2", 0, u_loaded)
            load_matrix(sp, d_place, "w_down_2", 0, d_loaded)

            def store_window(q, count, slots):
                for h in range(2):
                    sp.wait_ge(y_ev[q][h], count + 2 - q)
                sp.dma_start(ys[slots, :], yE).then_inc(y_stored[q], 16)

            def store_expert(e):
                start = start_of(sp, e)
                n_more, before_more = more_windows(sp, e)
                store_window(0, e, window(start, 0))
                with sp.If(n_more > 0), sp.Fori(0, n_more) as w:
                    store_window(1, before_more + w, window(start, w + 1))

            def load_after(e):
                sp.wait_ge(u_lo[1], e + 1)
                load_matrix(sp, u_place, "w_up_2", e + 1, u_loaded)
                sp.wait_ge(d_lo[0], e + 1)
                sp.wait_ge(d_lo[1], e + 1)
                load_matrix(sp, d_place, "w_down_2", e + 1, d_loaded)

            sp.wait_ge(info_ready, 1)
            with sp.Fori(0, N_EXP // 2 - 1) as j:
                for s in range(2):
                    e = 2 * j + s
                    load_after(e)
                    store_expert(e)
                    sp.wait_ge(g_used, e + 1)
                    load_matrix(sp, g_place[s], "w_gate_2", e + 2, g_loaded[s])
            load_after(N_EXP - 2)
            store_expert(N_EXP - 2)
            store_expert(N_EXP - 1)
            sp.wait_ge(y_stored[0], 16 * N_EXP + 16)
            sp.wait_ge(g_used, N_EXP)
            sp.dma_start(ystok, ys[0:SLOTS, :].rearrange("(s p) f -> p s f", p=P)).then_inc(ystok_in, 16)
            sp.wait_ge(fin_ev, 4)
            sp.dma_start(out[0].rearrange("(c p) f -> p c f", p=P), otok).then_inc(stored, 16)
            sp.wait_ge(stored, 16)

        @block.gpsimd
        def _(pool):
            rows = [
                (rows_a, R_MIX, a["mix_norm"].rearrange("l (k p) -> (l k) p", p=P)),
                (rows_a, R_FFN, a["ffn_norm"].rearrange("l (k p) -> (l k) p", p=P)),
                (rows_a, R_BIN, a["lru_b_in"].rearrange("l (k p) -> (l k) p", p=P)),
                (rows_a, R_CW, a["lru_conv_w"][0].rearrange("w (k p) -> (w k) p", p=P)),
                (rows_a, R_CB, a["lru_conv_b"].rearrange("l (k p) -> (l k) p", p=P)),
                (rows_a, R_GB, a["lru_gate_b"][0].rearrange("g (k p) -> (g k) p", p=P)),
                (rows_a, R_LAM, a["lru_lambda"].rearrange("l (k p) -> (l k) p", p=P)),
                (rows_a, R_BOUT, a["lru_b_out"].rearrange("l (k p) -> (l k) p", p=P)),
                (rows_a, R_FIN1, a["final_norm"].rearrange("(k p) -> k p", p=P)),
                (rows_b, R_N1, a["norm1_g_2"].rearrange("l (k p) -> (l k) p", p=P)),
                (rows_b, R_N2, a["norm2_g_2"].rearrange("l (k p) -> (l k) p", p=P)),
                (rows_b, R_FIN, a["final_g_2"].rearrange("(k p) -> k p", p=P)),
                (rows_b, R_ADA, a["b_ada_2"].rearrange("l (k p) -> (l k) p", p=P)),
                (rows_b, R_SUB, a["diff_subln_g_2"]),
                (rows_b, R_C, a["c_2"].rearrange("l (k p) -> (l k) p", p=P)),
            ]
            pool.dma_start(cst[:], a["constants"]).then_inc(const_in, 16)
            for dst, r, src in rows:
                pool.dma_start(dst[r:r + src.shape[0], :], src).then_inc(rows_in, 16)
            pool.dma_start(bias36[:, 0:N_GRP], a["b_group_2"].to_broadcast([P, N_GRP])).then_inc(lam_in, 16)
            pool.dma_start(bias36[:, N_GRP:], a["b_expert_2"].to_broadcast([P, N_EXP])).then_inc(lam_in, 16)
            for i, n in enumerate(("lambda_q1_2", "lambda_k1_2", "lambda_q2_2", "lambda_k2_2")):
                pool.dma_start(small[:, i * HD:(i + 1) * HD], a[n].to_broadcast([P, HD])).then_inc(lam_in, 16)
            for u in range(12):
                if u >= 2:
                    pool.wait_ge(ada_used, u - 1)
                dst = ring_b[:, (u % 2) * UNIT:(u % 2 + 1) * UNIT].rearrange("p (k f) -> p k f", k=KC)
                pool.dma_start(dst, a["w_ada_2"][0][:, u * 512:(u + 1) * 512].rearrange("(k p) n -> p k n", p=P)).then_inc(ada_loaded[u % 2], 16)
            for h in range(HEADS):
                pool.wait_ge(w_exp, h + 1)
                nc.gpsimd.tensor_tensor(sk_e[h % 2], sk_e[h % 2], stick, ALU.mult).then_inc(w_done, 1)
            pool.wait_ge(x_ready, 4 * 7)
            pool.dma_start(w_route[:, :, 0:N_GRP], a["w_group_2"][0].rearrange("(k p) n -> p k n", p=P)).then_inc(route_in, 16)
            pool.dma_start(w_route[:, :, N_GRP:], a["w_expert_2"][0].rearrange("(k p) n -> p k n", p=P)).then_inc(route_in, 16)
            pool.dma_start(slot_no, a["slot_numbers"]).then_inc(slotno_in, 16)
            pool.wait_ge(gather_ev, KC + 1)
            pool.wait_ge(combT_ev, 2)
            pool.wait_ge(info_ready, 1)

            def rows_of(q, slots):
                nc.gpsimd.tensor_copy(xw, xs[:, :, slots]).then_inc(xw_ready[q], 1)
                nc.gpsimd.tensor_copy(xp[0], xs[:, :, slots])
                pool.drain()
                nc.gpsimd.tensor_tensor(xp[1], xw, xp[0].bitcast(F32), ALU.subtract).then_inc(xp_ready[q], 1)

            with pool.Fori(0, N_EXP) as e:
                start = start_of(pool, e)
                n_more, before_more = more_windows(pool, e)
                pool.wait_ge(up_done[0][1], e + 1)
                rows_of(0, window(start, 0))
                pool.wait_ge(d_hi[1], e + 1)
                nc.gpsimd.tensor_tensor(d_part[1][:, 2:4], d_place[:, 2:4], d_part[0][:, 2:4].bitcast(F32), ALU.subtract).then_inc(d_lo[1], 1)
                with pool.If(n_more > 0), pool.Fori(0, n_more) as w:
                    pool.wait_ge(up_done[0][1], e + 2)
                    rows_of(1, window(start, w + 1))
                    pool.wait_ge(y_stored[1], 16 * (before_more + w) + 16)

        @block.scalar
        def _(act):
            n_chain = [0]

            def link(ins):
                n_chain[0] += 1
                ins.then_inc(act_ch, 1)
                act.wait_ge(act_ch, n_chain[0])

            def norm_square(n):
                for b in range(4):
                    act.wait_ge(x_ready, 4 * n + b + 1)
                    nc.scalar.activation(hT[:, 2 * b:2 * b + 2], xT[:, 2 * b:2 * b + 2], ACT.Square).then_inc(sq_done, 1)

            def norm_root(n):
                act.wait_ge(ms_done, n + 1)
                nc.scalar.activation(rstd[:], rstd[:], ACT.Sqrt).then_inc(root_done, 1)

            def norm_shift(n, shift):
                for k in range(KC):
                    act.wait_ge(h_part, KC * (n - 3) + k + 1)
                    nc.scalar.activation(hT[:, k], hT[:, k], ACT.Identity, bias=ada[:, shift + k:shift + k + 1]).then_inc(h_ready, 1)

            def copy_pair(name, dst, func=ACT.Copy):
                wait_tile(act, name)
                nc.scalar.activation(dst, bank(name), func).then_inc(evac_sem(name), 1)

            lam = cols[:, R_LAM:R_LAM + 8]
            act.wait_ge(setup_ev, 2)
            nc.scalar.activation(small[:, 256:264], cols[:, N_ROWS_A + R_C:N_ROWS_A + R_C + 8], ACT.Silu).then_inc(mod_ready, 1)
            link(nc.scalar.activation(small[:, 272:280], lam, ACT.Abs))
            link(nc.scalar.activation(small[:, 272:280], small[:, 272:280], ACT.Exp, scale=-1.0))
            nc.scalar.activation(small[:, 272:280], small[:, 272:280], ACT.Ln, bias=1.0).then_inc(sp8_ready, 1)

            norm_square(0)
            norm_root(0)
            act.wait_ge(pad_zero, 1)
            for i in range(4):
                wait_tile(act, f"rec{i}")
                for d in range(2):
                    m = 2 * i + d
                    ins = nc.scalar.activation(rec[:, m, 3:], bank(f"rec{i}")[:, d * 256:(d + 1) * 256], ACT.Identity, bias=col(R_BIN + 8 + m))
                ins.then_inc(evac_sem(f"rec{i}"), 1)
            for i in range(4):
                wait_tile(act, f"gb{i}")
                for d in range(2):
                    m = 2 * i + d
                    ins = nc.scalar.activation(gl[:, m], bank(f"gb{i}")[:, d * 256:(d + 1) * 256], ACT.Gelu_apprx_tanh, bias=col(R_BIN + m))
                ins.then_inc(evac_sem(f"gb{i}"), 1)
            for n in range(4):
                for g in range(2):
                    name = f"gate{n}_{g}"
                    wait_tile(act, name)
                    for d in range(2):
                        m = 2 * n + d
                        dst = (hT, ib)[g][:, m]
                        ins = nc.scalar.activation(dst, bank(name)[:, d * 256:(d + 1) * 256], ACT.Sigmoid, bias=col(R_GB + 8 * g + m))
                    ins.then_inc(evac_sem(name), 1)
            act.wait_ge(sp8_ready, 2)
            act.wait_ge(conv_done, 2)
            wait_evac(act, "gate3_0")
            for hf in range(2):
                for m in range(HALF * hf, HALF * hf + HALF):
                    nc.scalar.activation(tb[:, m], hT[:, m], ACT.Tanh, scale=small[:, 280 + m:281 + m])
                    ins = nc.scalar.activation(hT[:, m], hT[:, m], ACT.Exp, scale=small[:, 288 + m:289 + m])
                ins.then_inc(ta_done, 1)
            for hf in range(2):
                act.wait_ge(ratio_done, hf + 1)
                half = tb[:, HALF * hf:HALF * hf + HALF]
                nc.scalar.activation(half, half, ACT.Sqrt, scale=2.0).then_inc(mult_done, 1)

            def split_g(slot, loads):
                act.wait_ge(fi_loaded[slot], 32 * loads)
                nc.scalar.activation(fg_part[0], ffn_views(slot)[0], ACT.Copy).then_inc(fg_hi, 1)

            def split_u(slot):
                nc.scalar.activation(fu_part[0], ffn_views(slot)[1], ACT.Copy).then_inc(fu_hi, 1)

            def ffn_norm(n, layer):
                norm_square(n)
                split_g(0, ffn_loads(layer, 0))
                norm_root(n)
                for k in range(KC):
                    act.wait_ge(h_part, KC * layer + k + 1)
                    nc.scalar.activation(h_part_of[0][:, k], hT[:, k], ACT.Copy).then_inc(fh_hi, 1)
                split_u(0)

            def ffn(layer):
                base = layer * FFN_STEPS
                summed = summed_by(f"ffn{layer}_0")

                def step(s, n, loads, next_loads, before=True):
                    if next_loads is not None:
                        act.wait_ge(ffn_g, n + 1)
                        split_g(1 - s, next_loads)
                    act.wait_ge(ffn_gu, n + 1)
                    nc.scalar.activation(hid[:, s], ps[:, 2 * s, :], ACT.Silu).then_inc(ffn_silu, 1)
                    if next_loads is not None:
                        split_u(1 - s)
                    act.wait_ge(fo_loaded[s], 16 * loads)
                    if before:
                        act.wait_ge(unit_summed, n - base + summed - 1)
                    nc.scalar.activation(fd_part[0], ffn_views(s)[2], ACT.Copy).then_inc(fd_hi, 1)

                step(0, base, ffn_loads(layer, 0), ffn_loads(layer, 1), before=False)
                with act.Fori(0, (FFN_STEPS - 3) // 2) as j:
                    step(1, 2 * j + base + 1, j + ffn_loads(layer, 1), j + ffn_loads(layer, 2))
                    step(0, 2 * j + base + 2, j + ffn_loads(layer, 2), j + ffn_loads(layer, 3))
                step(1, base + FFN_STEPS - 2, ffn_loads(layer, FFN_STEPS - 2), ffn_loads(layer, FFN_STEPS - 1))
                step(0, base + FFN_STEPS - 1, ffn_loads(layer, FFN_STEPS - 1), None)

            ffn_norm(1, 0)
            ffn(0)

            norm_square(2)
            norm_root(2)
            for nm, dst in (("q", qT), ("k", kT)):
                for i in range(4):
                    copy_pair(f"{nm}{i}", dst[:, 2 * i:2 * i + 2])
            for i in range(4):
                copy_pair(f"v{i}", vtok[:, i % 2, (i // 2) * 512:(i // 2 + 1) * 512])

            def soft(h):
                b = h % 2
                act.wait_ge(z_done, h + 1)
                if h >= 2:
                    act.wait_ge(o_done, h - 1)
                link(nc.scalar.activation(sk_e[b], ps[:, b, 0:384], ACT.Abs, scale=SCALE))
                link(nc.scalar.activation(sk_e[b], sk_e[b], ACT.Exp, scale=-1.0))
                nc.scalar.activation(sk_e[b], sk_e[b], ACT.Ln, bias=1.0).then_inc(soft_done, 1)

            def weights(h):
                act.wait_ge(arg_done, h + 1)
                nc.scalar.activation(sk_e[h % 2], sk_t[h % 2], ACT.Exp).then_inc(w_exp, 1)

            def o_copy(c):
                act.wait_ge(o_done, 2 * c + 2)
                nc.scalar.activation(hT[:, c], ps[:, 4 + c % 2, 0:256], ACT.Copy).then_inc(o_evac, 1)

            soft(0)
            for h in range(HEADS):
                if h + 1 < HEADS:
                    soft(h + 1)
                weights(h)
                if h % 2 == 1 and h >= 3:
                    o_copy(h // 2 - 1)
            o_copy(7)
            ffn_norm(3, 1)
            ffn(1)

            norm_square(4)
            norm_root(4)
            norm_square(5)
            norm_root(5)
            norm_shift(5, 0)
            copy_pair("qm0", qm[:, 0:2])
            copy_pair("qm1", qm[:, 2:4])
            copy_pair("km0", km[:, 0:2])
            copy_pair("km1", km[:, 2:4])
            copy_pair("vm0", vm[:, 0])
            copy_pair("vm1", vm[:, 1])
            copy_pair("qd0", qd[:, 0:2])
            copy_pair("qd1", qd[:, 2:4])
            copy_pair("kd0", kd[:, 0:2])
            copy_pair("kd1", kd[:, 2:4])
            copy_pair("vd0", vd[:, 0])
            copy_pair("vd1", vd[:, 1])
            act.wait_ge(mod_ready, 4)
            nc.scalar.activation(small[:, 300:302], small[:, 298:300], ACT.Exp).then_inc(mod_ready, 1)

            def expo(s):
                act.wait_ge(s_max, s + 1)
                p, m, t = pbuf[s % 2], 304 + 4 * (s % 2), 312 + 4 * (s % 2)
                nc.scalar.activation(p[:, 0:128], p[:, 0:128], ACT.Exp, bias=small[:, m:m + 1], accum_out=small[:, t:t + 1])
                nc.scalar.activation(p[:, 128:384], p[:, 128:384], ACT.Exp, bias=small[:, m + 1:m + 2],
                                     accum_out=small[:, t + 1:t + 2]).then_inc(p_exp, 1)

            def pt_copy(u):
                act.wait_ge(t_done, u + 1)
                if u >= 2:
                    act.wait_ge(av_done, u - 1)
                nc.scalar.activation(ptb[u % 2], ps[:, 6, 0:384], ACT.Copy).then_inc(pt_evac, 1)

            def av_copy(u):
                act.wait_ge(av_done, u + 1)
                dst = qm[:, u // 2] if u < 8 else qd[:, u - 8]
                nc.scalar.activation(dst, ps[:, 7, 0:256], ACT.Copy).then_inc(av_evac, 1)

            def gate(name, dst):
                wait_tile(act, name)
                nc.scalar.activation(dst, bank(name), ACT.Sigmoid).then_inc(evac_sem(name), 1)

            expo(0)
            for u in range(12):
                if u + 1 < 8:
                    expo(u + 1)
                if u >= 8:
                    expo(2 * u - 8)
                    expo(2 * u - 7)
                pt_copy(u)
                if u < 8 and u % 2 == 1:
                    gate(f"gm{u // 2}", gm[:, u - 1:u + 1])
                if u >= 8:
                    gate(f"gd{u - 8}", gd[:, 2 * u - 16:2 * u - 14])
                if u >= 8 or u % 2 == 1:
                    av_copy(u)
            act.wait_ge(av_evac, 8)
            nc.scalar.activation(fm(0, 4), qd, ACT.Square).then_inc(osq_done, 1)
            act.wait_ge(oms_done, 1)
            nc.scalar.activation(fm(0, 4), fm(0, 4), ACT.Sqrt).then_inc(oroot_done, 1)

            norm_square(6)
            norm_root(6)
            norm_shift(6, 24)
            for c in range(TC):
                act.wait_ge(gmax_done, 1)
                ins = nc.scalar.activation(small[:, 100 + 4 * c:104 + 4 * c], small[:, 36 * c:36 * c + 4], ACT.Exp,
                                           bias=small[:, 96 + c:97 + c], accum_out=small[:, 110 + c:111 + c])
            ins.then_inc(gexp_done, 1)
            act.wait_ge(m2_ready, 1)
            nc.scalar.activation(small[:, 114:116], small[:, 112:114], ACT.Exp).then_inc(e2_done, 1)
            for q in range(4):
                act.wait_ge(htok_pe, q + 1)
                nc.scalar.activation(h2tok[:, q // 2, (q % 2) * 512:(q % 2 + 1) * 512], ps[:, q, :], ACT.Copy).then_inc(htok_ev, 1)
            for k in range(KC):
                act.wait_ge(gather_pe, k + 1)
                nc.scalar.activation(xs[:, k, 0:SLOTS], ps[:, k % 4, :], ACT.Copy).then_inc(gather_ev, 1)
            for q in range(2):
                act.wait_ge(combT_pe, q + 1)
                nc.scalar.activation(combT[:, 2 * q:2 * q + 2], ps[:, 4 + q, :], ACT.Copy).then_inc(combT_ev, 1)

            act.wait_ge(info_ready, 1)

            def act_window(q, count, e):
                act.wait_ge(gate_done[q], count + 1)
                nc.scalar.activation(hidE, ps[0:WIN, 0, :], ACT.Silu).then_inc(silu_done[q], 1)
                act.wait_ge(down_done[q][0], count + 1)
                act.wait_ge(y_stored[0], 16 * e + 16 * (q + 1))
                nc.scalar.activation(yE[:, 0:512], ps[0:WIN, 4, :], ACT.Copy).then_inc(y_ev[q][0], 1)

            def expert(e):
                nc.scalar.activation(small[:, 264:265], small[:, 256:257], ACT.Silu)
                act.wait_ge(u_loaded, 16 * e + 16)
                for h in range(2):
                    cols_h = slice(h * 256, (h + 1) * 256)
                    nc.scalar.activation(u_part[0][:, :, cols_h], u_place[:, :, cols_h], ACT.Copy).then_inc(u_hi[h], 1)
                act.wait_ge(d_loaded, 16 * e + 16)
                for h in range(2):
                    nc.scalar.activation(d_part[0][:, 2 * h:2 * h + 2], d_place[:, 2 * h:2 * h + 2], ACT.Copy).then_inc(d_hi[h], 1)
                n_more, before_more = more_windows(act, e)
                act_window(0, e, e)
                with act.If(n_more > 0), act.Fori(0, n_more) as w:
                    act_window(1, before_more + w, e)
                    act.wait_ge(y_stored[1], 16 * (before_more + w) + 16)
                act.wait_ge(up_done[0][1], e + 2)
                act.sem_inc(g_used, 1)
                act.wait_ge(down_done[0][1], e + 1)

            nc.scalar.nop().then_inc(y_ev[0][0], 1)
            nc.scalar.nop().then_inc(y_stored[0], 16)
            with act.Fori(0, N_EXP) as e:
                expert(e)
            norm_square(7)
            norm_root(7)
            for q in range(4):
                act.wait_ge(fin_pe, q + 1)
                nc.scalar.activation(otok[:, q // 2, (q % 2) * 512:(q % 2 + 1) * 512], ps[:, q, :], ACT.Copy).then_inc(fin_ev, 1)

        @block.vector
        def _(dve):
            n_chain = [0]

            def link(ins):
                n_chain[0] += 1
                ins.then_inc(dve_ch, 1)
                dve.wait_ge(dve_ch, n_chain[0])

            def norm_scale(n, gains, done=h_part):
                dst = xT if done is x_ready else hT
                dve.wait_ge(sum_done, n + 1)
                nc.vector.tensor_scalar(rstd[:], ps[:, SUM_BANK[n], 0:SEQ], 1.0 / D, EPS, ALU.mult, ALU.add).then_inc(ms_done, 1)
                dve.wait_ge(root_done, n + 1)
                link(nc.vector.reciprocal(rstd[:], rstd[:]))
                for k in range(KC):
                    ins = nc.vector.scalar_tensor_tensor(out=dst[:, k], in0=xT[:, k], scalar=gains(k), in1=rstd[:], op0=ALU.mult, op1=ALU.mult)
                    if done is not x_ready or k % 2 == 1:
                        ins.then_inc(done, 1)

            for q in range(4):
                dve.wait_ge(setup_pe, q + 1)
                ins = nc.vector.tensor_copy(xT[:, 2 * q:2 * q + 2], ps[:, q, :].rearrange("p (k t) -> p k t", k=2))
                ins.then_inc(x_ready, 1)
            dve.wait_ge(setup_pe, 5)
            nc.vector.tensor_copy(cols[:, 0:N_ROWS_A], ps[:, 4, 0:N_ROWS_A]).then_inc(setup_ev, 1)
            dve.wait_ge(setup_pe, 6)
            nc.vector.tensor_copy(cols[:, N_ROWS_A:], ps[:, 5, 0:N_ROWS_B]).then_inc(setup_ev, 1)
            dve.wait_ge(setup_ev, 2)
            nc.vector.memset(rec[:, :, 0:3], 0.0).then_inc(pad_zero, 1)
            norm_scale(0, lambda k: col(R_MIX + k), h_ready)

            dve.wait_ge(sp8_ready, 1)
            link(nc.vector.tensor_scalar(small[:, 280:288], cols[:, R_LAM:R_LAM + 8], -1.0, 0.0, ALU.mult, ALU.max))
            link(nc.vector.tensor_tensor(small[:, 280:288], small[:, 280:288], small[:, 272:280], ALU.add))
            link(nc.vector.tensor_scalar(small[:, 280:288], small[:, 280:288], 8.0, None, ALU.mult))
            nc.vector.tensor_scalar(small[:, 288:296], small[:, 280:288], -1.0, None, ALU.mult).then_inc(sp8_ready, 1)

            for hf in range(2):
                ms = range(HALF * hf, HALF * hf + HALF)
                wait_evac(dve, f"rec{2 * hf}")
                wait_evac(dve, f"rec{2 * hf + 1}")
                for m in ms:
                    ins = nc.vector.tensor_scalar(cv[:, m], rec[:, m, 3:3 + SEQ], col(R_CW + 24 + m), col(R_CB + m), ALU.mult, ALU.add)
                link(ins)
                for j in range(3):
                    for m in ms:
                        ins = nc.vector.scalar_tensor_tensor(out=cv[:, m], in0=rec[:, m, j:j + SEQ], scalar=col(R_CW + 8 * j + m),
                                                             in1=cv[:, m], op0=ALU.mult, op1=ALU.add)
                    if j < 2:
                        link(ins)
                ins.then_inc(conv_done, 1)
            for hf in range(2):
                hs = slice(HALF * hf, HALF * hf + HALF)
                wait_evac(dve, f"gate{2 * hf}_1")
                wait_evac(dve, f"gate{2 * hf + 1}_1")
                dve.wait_ge(conv_done, 2)
                link(nc.vector.tensor_tensor(ib[:, hs], ib[:, hs], cv[:, hs], ALU.mult))
                dve.wait_ge(tile_done, TILE_NO["gate3_1"] + 1)
                dve.wait_ge(ta_done, hf + 1)
                link(nc.vector.tensor_scalar(cv[:, hs], tb[:, hs], 1.0, None, ALU.add))
                link(nc.vector.reciprocal(cv[:, hs], cv[:, hs]))
                link(nc.vector.tensor_tensor(tb[:, hs], tb[:, hs], cv[:, hs], ALU.mult))
                nc.vector.tensor_scalar(tb[:, hs], tb[:, hs], 1e-30, None, ALU.max).then_inc(ratio_done, 1)
            for hf in range(2):
                hs = slice(HALF * hf, HALF * hf + HALF)
                dve.wait_ge(mult_done, hf + 1)
                link(nc.vector.tensor_tensor(ib[:, hs], ib[:, hs], tb[:, hs], ALU.mult))
                for m in range(HALF * hf, HALF * hf + HALF):
                    ins = nc.vector.tensor_tensor_scan(cv[:, m], hT[:, m], ib[:, m], 0.0, ALU.mult, ALU.add)
                link(ins)
                for m in range(HALF * hf, HALF * hf + HALF):
                    nc.vector.tensor_tensor(gl[:, m], gl[:, m], cv[:, m], ALU.mult).then_inc(y_done, 1)
            wait_used(dve, "lo1")
            for k in range(KC):
                ins = nc.vector.scalar_tensor_tensor(out=xT[:, k], in0=ps[:, 4 + k // 2, (k % 2) * 256:(k % 2 + 1) * 256], scalar=col(R_BOUT + k),
                                                     in1=xT[:, k], op0=ALU.add, op1=ALU.add)
                if k % 2 == 1:
                    ins.then_inc(x_ready, 1)

            def add_residual(last):
                wait_used(dve, last)
                for b in range(4):
                    ins = nc.vector.tensor_tensor(xT[:, 2 * b:2 * b + 2], ps[:, 4 + b, :].rearrange("p (k t) -> p k t", k=2), xT[:, 2 * b:2 * b + 2], ALU.add)
                    ins.then_inc(x_ready, 1)

            def subtract(lo, whole, hi, hi_sem, count, done):
                dve.wait_ge(hi_sem, count)
                nc.vector.tensor_tensor(lo, whole, hi.bitcast(F32), ALU.subtract).then_inc(done, 1)

            def split_g(slot, n):
                subtract(fg_part[1], ffn_views(slot)[0], fg_part[0], fg_hi, n + 1, fg_lo)

            def split_u(slot, n):
                subtract(fu_part[1], ffn_views(slot)[1], fu_part[0], fu_hi, n + 1, fu_lo)

            def ffn_norm(n, layer, gains):
                split_g(0, layer * FFN_STEPS)
                norm_scale(n, gains)
                for k in range(KC):
                    subtract(h_part_of[1][:, k], hT[:, k], h_part_of[0][:, k], fh_hi, KC * layer + k + 1, fh_lo)
                nc.vector.nop().then_inc(h_ready, KC)
                split_u(0, layer * FFN_STEPS)

            def ffn(layer):
                base = layer * FFN_STEPS

                def step(s, n, following=True):
                    if following:
                        split_g(1 - s, n + 1)
                    dve.wait_ge(ffn_silu, n + 1)
                    nc.vector.tensor_tensor(hid[:, s], hid[:, s], ps[:, 2 * s + 1, :], ALU.mult).then_inc(ffn_hid, 1)
                    dve.wait_ge(ffn_hid, n + 1)
                    nc.vector.tensor_copy(hid_part[s][0], hid[:, s]).then_inc(ffn_hid_hi, 1)
                    subtract(hid_part[s][1], hid[:, s], hid_part[s][0], ffn_hid_hi, n + 1, ffn_hid_lo)
                    if following:
                        split_u(1 - s, n + 1)
                    subtract(fd_part[1], ffn_views(s)[2], fd_part[0], fd_hi, n + 1, fd_lo)

                step(0, base)
                with dve.Fori(0, (FFN_STEPS - 3) // 2) as j:
                    step(1, 2 * j + base + 1)
                    step(0, 2 * j + base + 2)
                step(1, base + FFN_STEPS - 2)
                step(0, base + FFN_STEPS - 1, following=False)

            ffn_norm(1, 0, lambda k: col(R_FFN + k))
            ffn(0)
            add_residual(f"ffn0_{FFN_STEPS - 1}")

            norm_scale(2, lambda k: col(R_MIX + KC + k), h_ready)
            dve.wait_ge(mod_ready, 1)
            for u in range(12):
                w = ring_b[:, (u % 2) * UNIT:(u % 2 + 1) * UNIT].rearrange("p (k f) -> p k f", k=KC)
                dve.wait_ge(ada_loaded[u % 2], 16 * (u // 2 + 1))
                acc = ada_acc[:, u % 2]
                if u >= 2:
                    dve.wait_ge(ada_psum, u - 1)
                link(nc.vector.tensor_scalar(acc, w[:, 0], small[:, 256:257], None, ALU.mult))
                for k in range(1, KC):
                    ins = nc.vector.scalar_tensor_tensor(out=acc, in0=w[:, k], scalar=small[:, 256 + k:257 + k], in1=acc, op0=ALU.mult, op1=ALU.add)
                    if k < KC - 1:
                        link(ins)
                ins.then_inc(ada_used, 1)
            dve.wait_ge(ada_psum, 12)
            link(nc.vector.tensor_tensor(ada[:], ps[:, 6, 0:48], cols[:, N_ROWS_A + R_ADA:N_ROWS_A + R_ADA + 48], ALU.add))
            link(nc.vector.scalar_tensor_tensor(out=gain[:, 0], in0=ada[:, 8:16], scalar=1.0, in1=cols[:, N_ROWS_A + R_N1:N_ROWS_A + R_N1 + 8],
                                                op0=ALU.add, op1=ALU.mult))
            nc.vector.scalar_tensor_tensor(out=gain[:, 1], in0=ada[:, 32:40], scalar=1.0, in1=cols[:, N_ROWS_A + R_N2:N_ROWS_A + R_N2 + 8],
                                           op0=ALU.add, op1=ALU.mult).then_inc(mod_ready, 1)

            def soft_mask(h):
                b = h % 2
                dve.wait_ge(soft_done, h + 1)
                if h >= 2:
                    dve.wait_ge(suf_done, h - 1)
                    dve.wait_ge(w_exp, h - 1)
                link(nc.vector.tensor_scalar(sk_p[b], ps[:, b, 0:384], SCALE, 0.0, ALU.mult, ALU.max))
                link(nc.vector.tensor_tensor(sk_p[b], sk_p[b], sk_e[b], ALU.add))
                link(nc.vector.scalar_tensor_tensor(out=sk_t[b], in0=ps[:, b, 0:384], scalar=SCALE, in1=sk_p[b], op0=ALU.mult, op1=ALU.subtract))
                nc.vector.tensor_tensor(sk_p[b], sk_p[b], stick, ALU.mult).then_inc(spm_done, 1)

            def argument(h):
                b = h % 2
                dve.wait_ge(suf_done, h + 1)
                nc.vector.tensor_tensor(sk_t[b], sk_t[b], ps[:, 2 + b, 0:384], ALU.subtract).then_inc(arg_done, 1)

            soft_mask(0)
            for h in range(HEADS):
                if h + 1 < HEADS:
                    soft_mask(h + 1)
                argument(h)
            add_residual("wo1")
            ffn_norm(3, 1, lambda k: col(R_FFN + KC + k))
            ffn(1)
            add_residual(f"ffn1_{FFN_STEPS - 1}")

            norm_scale(4, lambda k: col(R_FIN1 + k), x_ready)
            dve.wait_ge(mod_ready, 2)
            dve.wait_ge(lam_in, 16 * 6)
            for i in range(2):
                link(nc.vector.tensor_tensor(small[:, 2 * i * HD:(2 * i + 1) * HD], small[:, 2 * i * HD:(2 * i + 1) * HD],
                                             small[:, (2 * i + 1) * HD:(2 * i + 2) * HD], ALU.mult))
                ins = nc.vector.reduce_sum(small[:, 298 + i:299 + i], small[:, 2 * i * HD:(2 * i + 1) * HD], AX_X)
                ins.then_inc(mod_ready, 1)
            norm_scale(5, lambda k: gain[:, 0, k:k + 1])

            dve.wait_ge(rope_in, 16)
            for i, (nm, x) in enumerate((("qm", qm), ("km", km), ("qd", qd), ("kd", kd))):
                for d in range(2):
                    r = 2 * i + d
                    xx = x[:, 2 * d:2 * d + 2]
                    t3 = rope_t.rearrange("p (k t) -> p k t", k=2)
                    u3 = rope_u.rearrange("p (k t) -> p k t", k=2)
                    wait_tile(dve, f"rot{r}")
                    for kk in range(2):
                        nc.vector.tensor_tensor(t3[:, kk], xx[:, kk], rope[:, 0:256], ALU.mult)
                        ins = nc.vector.tensor_tensor(u3[:, kk], bank(f"rot{r}")[:, kk * 256:(kk + 1) * 256], rope[:, 256:512], ALU.mult)
                    ins.then_inc(evac_sem(f"rot{r}"), 1)
                    wait_evac(dve, f"rot{r}")
                    ins = nc.vector.tensor_tensor(xx, t3, u3, ALU.add)
                    ins.then_inc(roped, 1)
                    dve.wait_ge(roped, r + 1)
            dve.wait_ge(mod_ready, 5)
            link(nc.vector.tensor_tensor(small[:, 302:303], small[:, 300:301], small[:, 301:302], ALU.subtract))
            link(nc.vector.tensor_scalar(small[:, 302:303], small[:, 302:303], LAM_INIT, None, ALU.add))

            def masked_max(s):
                b = s % 2
                p, m = pbuf[b], 304 + 4 * b
                dve.wait_ge(s_done, s + 1)
                if 2 <= s < 10:
                    dve.wait_ge(t_done, s - 1)
                elif s >= 10:
                    dve.wait_ge(t_done, (s - 8) // 2 + 8)
                link(nc.vector.scalar_tensor_tensor(out=p, in0=ps[:, 4 + b, 0:384], scalar=SCALE, in1=negm, op0=ALU.mult, op1=ALU.add))
                nc.vector.reduce_max(small[:, m:m + 1], p[:, 0:128], AX_X)
                link(nc.vector.reduce_max(small[:, m + 1:m + 2], p[:, 128:384], AX_X))
                nc.vector.tensor_scalar(small[:, m:m + 2], small[:, m:m + 2], -1.0, None, ALU.mult).then_inc(s_max, 1)

            def norm_head(u):
                b = u % 2
                dve.wait_ge(p_exp, u + 1)
                r = 312 + 4 * b
                link(nc.vector.reciprocal(small[:, r + 2:r + 4], small[:, r:r + 2]))
                p = pbuf[b]
                nc.vector.tensor_scalar(p[:, 0:128], p[:, 0:128], small[:, r + 2:r + 3], None, ALU.mult)
                nc.vector.tensor_scalar(p[:, 128:384], p[:, 128:384], small[:, r + 3:r + 4], None, ALU.mult).then_inc(p_norm, 1)

            def norm_diff(u):
                dve.wait_ge(p_exp, 8 + 2 * (u - 8) + 2)
                nc.vector.reciprocal(small[:, 314:316], small[:, 312:314])
                link(nc.vector.reciprocal(small[:, 318:320], small[:, 316:318]))
                link(nc.vector.tensor_scalar(small[:, 318:320], small[:, 318:320], small[:, 302:303], None, ALU.mult))
                nc.vector.tensor_scalar(pbuf[1][:, 0:128], pbuf[1][:, 0:128], small[:, 318:319], None, ALU.mult)
                link(nc.vector.tensor_scalar(pbuf[1][:, 128:384], pbuf[1][:, 128:384], small[:, 319:320], None, ALU.mult))
                for q, (lo, hi) in enumerate(((0, 128), (128, 384))):
                    ins = nc.vector.scalar_tensor_tensor(out=pbuf[0][:, lo:hi], in0=pbuf[0][:, lo:hi], scalar=small[:, 314 + q:315 + q],
                                                         in1=pbuf[1][:, lo:hi], op0=ALU.mult, op1=ALU.subtract)
                ins.then_inc(p_norm, 1)

            masked_max(0)
            for u in range(12):
                if u + 1 < 8:
                    masked_max(u + 1)
                if u < 8:
                    norm_head(u)
                else:
                    masked_max(2 * u - 8)
                    masked_max(2 * u - 7)
                    norm_diff(u)
            dve.wait_ge(osum_done, 1)
            link(nc.vector.tensor_scalar(flat(0, 1024), ps[:, 4:6, :].rearrange("p b n -> p (b n)"), 1.0 / P, EPS, ALU.mult, ALU.add))
            nc.vector.nop().then_inc(oms_done, 1)
            dve.wait_ge(oroot_done, 1)
            link(nc.vector.reciprocal(flat(0, 1024), flat(0, 1024)))
            link(nc.vector.tensor_scalar(small[:, 303:304], col(R_SUB, 1), 1.0 - LAM_INIT, None, ALU.mult))
            nc.vector.scalar_tensor_tensor(out=flat(WORK + 3072, 1024), in0=flat(WORK + 3072, 1024), scalar=small[:, 303:304], in1=flat(0, 1024),
                                           op0=ALU.mult, op1=ALU.mult).then_inc(on_ready, 1)
            for i in range(4):
                wait_tile(dve, f"ym{i}")
                wait_evac(dve, f"gm{i}")
                g2 = gm[:, 2 * i:2 * i + 2]
                nc.vector.tensor_tensor(g2, bank(f"ym{i}").rearrange("p (k t) -> p k t", k=2), g2, ALU.mult).then_inc(evac_sem(f"ym{i}"), 1)
            for i in range(4):
                wait_tile(dve, f"yd{i}")
                wait_evac(dve, f"gd{i}")
                wait_evac(dve, f"ym{i}")
                g2 = gd[:, 2 * i:2 * i + 2]
                nc.vector.tensor_tensor(g2, bank(f"yd{i}").rearrange("p (k t) -> p k t", k=2), g2, ALU.mult).then_inc(evac_sem(f"yd{i}"), 1)
                wait_evac(dve, f"yd{i}")
                nc.vector.tensor_tensor(gm[:, 2 * i:2 * i + 2], gm[:, 2 * i:2 * i + 2], g2, ALU.add).then_inc(merged_ready, 1)

            def gated_residual(at, bank0):
                for k in range(KC):
                    ins = nc.vector.scalar_tensor_tensor(out=xT[:, k], in0=ps[:, bank0 + k // 2, (k % 2) * 256:(k % 2 + 1) * 256],
                                                         scalar=ada[:, at + k:at + k + 1], in1=xT[:, k], op0=ALU.mult, op1=ALU.add)
                    if k % 2 == 1:
                        ins.then_inc(x_ready, 1)

            wait_used(dve, "out1")
            gated_residual(16, 4)

            norm_scale(6, lambda k: gain[:, 1, k:k + 1])
            dve.wait_ge(logit_done, 1)

            def sm(lo, n=1):
                return small[:, lo:lo + n]

            def both(f):
                for c in range(TC):
                    ins = f(c)
                link(ins)

            V = nc.vector
            LG, OHG, EM, O1, O2 = 0, 80, 120, 160, 224
            both(lambda c: V.tensor_tensor(sm(LG + 36 * c, 36), ps[:, 4, 36 * c:36 * c + 36], bias36[:], ALU.add))
            both(lambda c: V.reduce_max(sm(94 + c), sm(LG + 36 * c, 4), AX_X))
            for c in range(TC):
                ins = V.tensor_scalar(sm(96 + c), sm(94 + c), -1.0, None, ALU.mult)
            ins.then_inc(gmax_done, 1)

            def first_max(src, n, top, dst, tmp):
                both(lambda c: V.tensor_scalar(sm(dst(c), n), sm(src(c), n), sm(top(c)), -64.0, ALU.is_equal, ALU.mult))
                both(lambda c: V.tensor_tensor(sm(dst(c), n), sm(dst(c), n), iota8[:, 0:n], ALU.add))
                both(lambda c: V.tensor_reduce(sm(tmp + c), sm(dst(c), n), AX_X, ALU.min))
                both(lambda c: V.tensor_scalar(sm(dst(c), n), sm(dst(c), n), sm(tmp + c), None, ALU.is_equal))

            first_max(lambda c: LG + 36 * c, 4, lambda c: 94 + c, lambda c: OHG + 4 * c, 116)
            both(lambda c: V.tensor_scalar(sm(EM + 8 * c, 8), sm(LG + 36 * c + 4, 8), sm(OHG + 4 * c), None, ALU.mult))
            for g in range(1, N_GRP):
                both(lambda c: V.scalar_tensor_tensor(out=sm(EM + 8 * c, 8), in0=sm(LG + 36 * c + 4 + 8 * g, 8), scalar=sm(OHG + 4 * c + g),
                                                      in1=sm(EM + 8 * c, 8), op0=ALU.mult, op1=ALU.add))
            both(lambda c: V.reduce_max(sm(118 + c), sm(EM + 8 * c, 8), AX_X))
            first_max(lambda c: EM + 8 * c, 8, lambda c: 118 + c, lambda c: 136 + 8 * c, 116)
            both(lambda c: V.scalar_tensor_tensor(out=sm(EM + 8 * c, 8), in0=sm(136 + 8 * c, 8), scalar=-3e38, in1=sm(EM + 8 * c, 8),
                                                  op0=ALU.mult, op1=ALU.add))
            both(lambda c: V.reduce_max(sm(152 + c), sm(EM + 8 * c, 8), AX_X))
            for c in range(TC):
                ins = V.tensor_tensor(sm(112 + c), sm(152 + c), sm(118 + c), ALU.subtract)
            ins.then_inc(m2_ready, 1)
            first_max(lambda c: EM + 8 * c, 8, lambda c: 152 + c, lambda c: EM + 8 * c, 116)
            dve.wait_ge(e2_done, 1)
            dve.wait_ge(gexp_done, 1)
            link(V.tensor_scalar(sm(154, 2), sm(114, 2), 1.0, None, ALU.add))
            link(V.tensor_tensor(sm(154, 2), sm(154, 2), sm(110, 2), ALU.mult))
            link(V.reciprocal(sm(154, 2), sm(154, 2)))
            link(V.tensor_tensor(sm(156, 2), sm(154, 2), sm(114, 2), ALU.mult))
            for g in range(N_GRP):
                for c in range(TC):
                    V.tensor_scalar(sm(O1 + 32 * c + 8 * g, 8), sm(136 + 8 * c, 8), sm(OHG + 4 * c + g), None, ALU.mult)
                    ins = V.tensor_scalar(sm(O2 + 32 * c + 8 * g, 8), sm(EM + 8 * c, 8), sm(OHG + 4 * c + g), None, ALU.mult)
            link(ins)
            V.tensor_tensor(sm(320, 64), sm(O1, 64), sm(O2, 64), ALU.add).then_inc(mask_ready, 1)
            dve.wait_ge(pos_done, 1)
            START = 0
            link(V.tensor_copy(sm(32, 32), ps[:, 5, 64:96]))
            link(V.tensor_tensor_scan(sm(START, 32), cst[:, C_ONES:C_ONES + 32], sm(32, 32), 0.0, ALU.mult, ALU.add))
            link(V.tensor_tensor(sm(START, 32), sm(START, 32), sm(32, 32), ALU.subtract))
            both(lambda c: V.tensor_tensor(sm(320 + 32 * c, 32), ps[:, 5, 32 * c:32 * c + 32], sm(START, 32), ALU.add))
            link(V.tensor_tensor(sm(O1, 64), sm(O1, 64), sm(320, 64), ALU.mult))
            link(V.tensor_tensor(sm(O2, 64), sm(O2, 64), sm(320, 64), ALU.mult))
            both(lambda c: V.reduce_sum(sm(384 + c), sm(O1 + 32 * c, 32), AX_X))
            both(lambda c: V.reduce_sum(sm(386 + c), sm(O2 + 32 * c, 32), AX_X))
            dve.wait_ge(slotno_in, 16)
            for c in range(TC):
                link(V.tensor_scalar(pick_t, slot_no, sm(384 + c), None, ALU.is_equal))
                link(V.scalar_tensor_tensor(out=pick[:, c], in0=slot_no, scalar=sm(386 + c), in1=pick_t, op0=ALU.is_equal, op1=ALU.add))
            V.nop().then_inc(pick_ready, 1)
            for c in range(TC):
                link(V.tensor_scalar(pick_t, slot_no, sm(384 + c), sm(154 + c), ALU.is_equal, ALU.mult))
                link(V.tensor_scalar(comb[:, c], slot_no, sm(386 + c), sm(156 + c), ALU.is_equal, ALU.mult))
                link(V.tensor_tensor(comb[:, c], comb[:, c], pick_t, ALU.add))
            V.nop().then_inc(comb_ready, 1)
            link(V.tensor_scalar(sm(96, 32), sm(32, 32), float(WIN), None, ALU.is_gt))
            for w in range(2, SEQ // WIN):
                link(V.scalar_tensor_tensor(out=sm(96, 32), in0=sm(32, 32), scalar=float(w * WIN), in1=sm(96, 32), op0=ALU.is_gt, op1=ALU.add))
            link(V.tensor_tensor_scan(sm(128, 32), cst[:, C_ONES:C_ONES + 32], sm(96, 32), 0.0, ALU.mult, ALU.add))
            link(V.tensor_tensor(sm(128, 32), sm(128, 32), sm(96, 32), ALU.subtract))
            V.tensor_copy(info[:, 0:32], small[0:1, 0:32])
            V.tensor_copy(info[:, 32:64], small[0:1, 96:128])
            V.tensor_copy(info[:, 64:96], small[0:1, 128:160]).then_inc(info_ready, 1)
            dve.wait_ge(gather_pe, KC)
            link(V.memset(xs[:, :, SLOTS:], 0.0))
            V.nop().then_inc(gather_ev, 1)

            dve.wait_ge(info_ready, 1)
            dve.wait_ge(combT_ev, 2)
            V.nop().then_inc(y_ev[0][1], 1)

            def dve_window(q, count, e):
                for h in range(2):
                    dve.wait_ge(silu_done[q], count + 1)
                    dve.wait_ge(up_done[q][h], count + 1 + (h if q == 0 else 0))
                    half = hidE[:, h * 256:(h + 1) * 256]
                    V.tensor_tensor(half, half, ps[0:WIN, 1 + h, 0:256], ALU.mult).then_inc(hid_done[q][h], 1)
                    dve.wait_ge(hidT_pe[q][h], count + 1)
                    turned = ps[:, 3 * (1 - h), 0:2 * WIN].rearrange("p (k s) -> p k s", k=2)
                    V.tensor_copy(hidT[0][:, 2 * h:2 * h + 2], turned).then_inc(hidT_hi[q][h], 1)
                    dve.wait_ge(hidT_hi[q][h], count + 1)
                    V.tensor_tensor(hidT[1][:, 2 * h:2 * h + 2], turned, hidT[0][:, 2 * h:2 * h + 2].bitcast(F32), ALU.subtract).then_inc(hidT_lo[q][h], 1)
                dve.wait_ge(down_done[q][1], count + 1)
                dve.wait_ge(y_stored[0], 16 * e + 16 * (q + 1))
                V.tensor_copy(yE[:, 512:1024], ps[0:WIN, 5, :]).then_inc(y_ev[q][1], 1)

            with dve.Fori(0, N_EXP) as e:
                for h in range(2):
                    cols_h = slice(h * 256, (h + 1) * 256)
                    dve.wait_ge(u_hi[h], e + 1)
                    V.tensor_tensor(u_part[1][:, :, cols_h], u_place[:, :, cols_h], u_part[0][:, :, cols_h].bitcast(F32), ALU.subtract).then_inc(u_lo[h], 1)
                dve.wait_ge(d_hi[0], e + 1)
                V.tensor_tensor(d_part[1][:, 0:2], d_place[:, 0:2], d_part[0][:, 0:2].bitcast(F32), ALU.subtract).then_inc(d_lo[0], 1)
                n_more, before_more = more_windows(dve, e)
                dve_window(0, e, e)
                with dve.If(n_more > 0), dve.Fori(0, n_more) as w:
                    dve_window(1, before_more + w, e)
                    dve.wait_ge(y_stored[1], 16 * (before_more + w) + 16)
            dve.wait_ge(y2_done, 1)
            gated_residual(40, 0)
            norm_scale(7, lambda k: col(R_FIN + k, 1), h_ready)

        @block.tensor
        def _(pe):
            mm = nc.tensor.matmul

            def norm_sums(n):
                for k in range(KC):
                    if k % 2 == 0:
                        pe.wait_ge(sq_done, 4 * n + k // 2 + 1)
                    ins = mm(ps[:, SUM_BANK[n], 0:SEQ], ones, hT[:, k], start=(k == 0), stop=(k == KC - 1))
                ins.then_inc(sum_done, 1)

            def start_tile(name):
                t = TILE_NO[name]
                if t >= 4:
                    pe.wait_ge(evac[t % 4], t // 4)
                return bank(name)

            def wait_rows(i, k):
                pe.wait_ge(h_ready, KC * i + k + 1)

            def product_pair(name, w, m, kn, rhs, norm=None):
                b = start_tile(name)
                for d in range(2):
                    for k in range(kn):
                        if norm is not None and d == 0:
                            wait_rows(norm, k)
                        ins = mm(b[:, d * 256:(d + 1) * 256], w[:, k, (m + d) * P:(m + d + 1) * P], rhs[:, k], start=(k == 0), stop=(k == kn - 1))
                ins.then_inc(tile_done, 1)

            def token_major(name, w, x, c):
                b = start_tile(name)
                for k in range(KC):
                    ins = mm(b, x[:, k, c * P:(c + 1) * P], w[:, k], start=(k == 0), stop=(k == KC - 1))
                ins.then_inc(tile_done, 1)

            def accumulate(w, kn, k_first, rhs, first, last):
                for k in range(kn):
                    r = rhs(k_first + k)
                    for f in range(KC):
                        ins = mm(ps[:, 4 + f // 2, (f % 2) * 256:(f % 2 + 1) * 256], w[:, k, f * P:(f + 1) * P], r,
                                 start=(first and k == 0 and f % 2 == 0), stop=(last and k == kn - 1), skip_group_check=True)
                return ins

            pe.wait_ge(const_in, 16)
            pe.wait_ge(xtok_in, 16)
            for q in range(4):
                for d in range(2):
                    for c in range(TC):
                        ins = nc.tensor.transpose(ps[:, q, d * 256 + c * P:d * 256 + (c + 1) * P], xtok[:, c, (2 * q + d) * P:(2 * q + d + 1) * P], ident)
                ins.then_inc(setup_pe, 1)
            pe.wait_ge(rows_in, 16 * 15)
            nc.tensor.transpose(ps[:, 4, 0:N_ROWS_A], rows_a[0:N_ROWS_A, :], ident[0:N_ROWS_A, 0:N_ROWS_A]).then_inc(setup_pe, 1)
            nc.tensor.transpose(ps[:, 5, 0:N_ROWS_B], rows_b[0:N_ROWS_B, :], ident[0:N_ROWS_B, 0:N_ROWS_B]).then_inc(setup_pe, 1)

            norm_sums(0)
            for nm in ("rec", "gb"):
                for u in range(2):
                    wait_unit(pe, f"{nm}{u}")
                    w = unit_view(f"{nm}{u}")
                    for h in range(2):
                        product_pair(f"{nm}{2 * u + h}", w, 2 * h, KC, hT, 0 if (nm, u, h) == ("rec", 0, 0) else None)
            pe.wait_ge(gates_in, 16 * 8)
            w = unit_view("gates")
            for n in range(4):
                if n % 2 == 0:
                    pe.wait_ge(conv_done, n // 2 + 1)
                for g in range(2):
                    b = start_tile(f"gate{n}_{g}")
                    for d in range(2):
                        for c in range(2):
                            ins = mm(b[:, d * 256:(d + 1) * 256], w[:, g, n, c, d * P:(d + 1) * P], cv[:, 2 * n + c], start=(c == 0), stop=(c == 1))
                    ins.then_inc(tile_done, 1)
            for u in range(2):
                wait_unit(pe, f"lo{u}")
                for k in range(4):
                    pe.wait_ge(y_done, 4 * u + k + 1)
                    ins = accumulate(unit_view(f"lo{u}")[:, k:k + 1], 1, 4 * u + k, lambda k: gl[:, k], u == 0 and k == 0, u == 1 and k == 3)
                ins.then_inc(unit_summed, 1)

            def ffn(layer):
                base = layer * FFN_STEPS

                def half(w, b, wait_rows):
                    for d in range(2):
                        for k in range(KC):
                            if wait_rows and d == 0:
                                pe.wait_ge(fh_lo, KC * layer + k + 1)
                            for i, (px, pw) in enumerate(PART_PAIRS):
                                ins = mm(ps[:, b, d * 256:(d + 1) * 256], w[pw][:, k, d * P:(d + 1) * P], h_part_of[px][:, k],
                                         start=(k == 0 and i == 0), stop=(k == KC - 1 and i == 2))
                    return ins

                def gate_up(slot, step, wait_rows=False):
                    pe.wait_ge(fg_lo, step + 1)
                    half(fg_part, 2 * slot, wait_rows).then_inc(ffn_g, 1)
                    pe.wait_ge(fu_lo, step + 1)
                    half(fu_part, 2 * slot + 1, False).then_inc(ffn_gu, 1)

                def down(slot, step, first=False, last=False):
                    pe.wait_ge(fd_lo, step + 1)
                    pe.wait_ge(ffn_hid_lo, step + 1)
                    for i, (px, pw) in enumerate(PART_PAIRS):
                        ins = accumulate(fd_part[pw], 2, 0, lambda k: hid_part[slot][px][:, k * 256:(k + 1) * 256], first and i == 0, last and i == 2)
                    ins.then_inc(unit_summed, 1)

                gate_up(0, base, wait_rows=True)
                gate_up(1, base + 1)
                down(0, base, first=True)
                with pe.Fori(0, (FFN_STEPS - 3) // 2) as j:
                    gate_up(0, 2 * j + base + 2)
                    down(1, 2 * j + base + 1)
                    gate_up(1, 2 * j + base + 3)
                    down(0, 2 * j + base + 2)
                gate_up(0, base + FFN_STEPS - 1)
                down(1, base + FFN_STEPS - 2)
                down(0, base + FFN_STEPS - 1, last=True)

            norm_sums(1)
            ffn(0)

            norm_sums(2)

            def ada_sum(u):
                pe.wait_ge(ada_used, u + 1)
                for j in range(4):
                    ins = mm(ps[:, 6, 4 * u + j:4 * u + j + 1], ada_acc[:, u % 2, j * P:(j + 1) * P], ones[:, 0:1], start=True, stop=True)
                ins.then_inc(ada_psum, 1)

            n_ada = 0
            for nm in ("q", "k"):
                for u in range(2):
                    wait_unit(pe, f"{nm}{u}")
                    for h in range(2):
                        product_pair(f"{nm}{2 * u + h}", unit_view(f"{nm}{u}"), 2 * h, KC, hT, 2 if (nm, u, h) == ("q", 0, 0) else None)
                        ada_sum(n_ada)
                        n_ada += 1
            for u in range(2):
                wait_unit(pe, f"v{u}")
                for c in range(TC):
                    token_major(f"v{2 * u + c}", unit_view(f"v{u}"), hT, c)
                    ada_sum(n_ada)
                    n_ada += 1
            for t in range(4):
                wait_evac(pe, f"v{t}")

            def scores(h):
                lo = (h % 2) * HD
                if h >= 2:
                    pe.wait_ge(spm_done, h - 1)
                q, k, b = qT[lo:lo + HD, h // 2], kT[lo:lo + HD, h // 2], ps[:, h % 2]
                mm(b[:, 0:256], k[:, 0:P], q, start=True, stop=True)
                mm(b[:, 256:384], k[:, P:], q[:, P:], start=True, stop=True).then_inc(z_done, 1)

            def suffix(h):
                b = ps[:, 2 + h % 2]
                pe.wait_ge(spm_done, h + 1)
                if h >= 2:
                    pe.wait_ge(arg_done, h - 1)
                mm(b[:, 0:384], after, sk_p[h % 2], start=True, stop=False, skip_group_check=True)
                mm(b[:, 128:256], ones, sk_p[h % 2][:, 256:384], start=False, stop=True, skip_group_check=True).then_inc(suf_done, 1)

            def values(h):
                lo, c = (h % 2) * HD, h // 2
                b = ps[lo:lo + HD, 4 + c % 2]
                pe.wait_ge(w_done, h + 1)
                if h >= 4 and h % 2 == 0:
                    pe.wait_ge(o_evac, c - 1)
                mm(b[:, 0:256], vtok[:, 0, h * HD:(h + 1) * HD], sk_e[h % 2][:, 0:256], start=True, stop=False, skip_group_check=True)
                mm(b[:, 128:256], vtok[:, 1, h * HD:(h + 1) * HD], sk_e[h % 2][:, 256:384], start=False, stop=True, skip_group_check=True).then_inc(o_done, 1)

            scores(0)
            scores(1)
            for h in range(HEADS):
                suffix(h)
                if h >= 1:
                    values(h - 1)
                if h + 2 < HEADS:
                    scores(h + 2)
            values(HEADS - 1)
            pe.wait_ge(o_evac, 8)
            for u in range(2):
                wait_unit(pe, f"wo{u}")
                ins = accumulate(unit_view(f"wo{u}"), 4, 4 * u, lambda k: hT[:, k], u == 0, u == 1)
                ins.then_inc(unit_summed, 1)

            norm_sums(3)
            ffn(1)

            norm_sums(4)
            norm_sums(5)
            for nm in ("qm", "km", "vm", "qd", "kd", "vd"):
                wait_unit(pe, nm)
                for h in range(2):
                    if nm[0] == "v":
                        token_major(f"{nm}{h}", unit_view(nm), hT, h)
                    else:
                        product_pair(f"{nm}{h}", unit_view(nm), 2 * h, KC, hT, 4 if (nm, h) == ("qm", 0) else None)
            for i, (nm, x) in enumerate((("qm", qm), ("km", km), ("qd", qd), ("kd", kd))):
                for d in range(2):
                    wait_evac(pe, f"{nm}{d}")
                    b = start_tile(f"rot{2 * i + d}")
                    for kk in range(2):
                        ins = mm(b[:, kk * 256:(kk + 1) * 256], rot, x[:, 2 * d + kk], start=True, stop=True)
                    ins.then_inc(tile_done, 1)

            def softmax_scores(s):
                q, k = (qm, km) if s < 8 else (qd, kd)
                c, lo = (s % 8) // 2, (s % 2) * HD
                b = ps[:, 4 + s % 2]
                if s >= 2:
                    pe.wait_ge(s_max, s - 1)
                mm(b[:, 0:128], q[lo:lo + HD, c, 0:P], k[lo:lo + HD, c, 0:P], start=True, stop=True)
                mm(b[:, 128:384], q[lo:lo + HD, c, P:], k[lo:lo + HD, c, :], start=True, stop=True).then_inc(s_done, 1)

            def next_scores(u):
                if u < 8:
                    softmax_scores(u)
                elif u < 12:
                    softmax_scores(2 * u - 8)
                    softmax_scores(2 * u - 7)

            def gate_tile(nm, i):
                if i % 2 == 0:
                    wait_unit(pe, f"{nm}{i // 2}")
                product_pair(f"{nm}{i}", unit_view(f"{nm}{i // 2}"), 2 * (i % 2), KC, hT)

            pe.wait_ge(roped, 8)
            wait_evac(pe, "vm1")
            next_scores(0)
            for u in range(12):
                next_scores(u + 1)
                p = pbuf[u % 2] if u < 8 else pbuf[0]
                pe.wait_ge(p_norm, u + 1)
                if u >= 1:
                    pe.wait_ge(pt_evac, u)
                for i in range(3):
                    ins = nc.tensor.transpose(ps[:, 6, i * P:(i + 1) * P], p[:, i * P:(i + 1) * P], ident)
                ins.then_inc(t_done, 1)
                if u < 8 and u % 2 == 1:
                    gate_tile("gm", u // 2)
                if u >= 8:
                    gate_tile("gd", u - 8)
                pe.wait_ge(pt_evac, u + 1)
                pt = ptb[u % 2]
                if u < 8:
                    b = ps[(u % 2) * HD:(u % 2 + 1) * HD, 7]
                    v0, v1 = vm[:, 0, u * HD:(u + 1) * HD], vm[:, 1, u * HD:(u + 1) * HD]
                    if u % 2 == 0 and u:
                        pe.wait_ge(av_evac, u // 2)
                else:
                    b = ps[:, 7]
                    v0, v1 = vd[:, 0, (u - 8) * P:(u - 7) * P], vd[:, 1, (u - 8) * P:(u - 7) * P]
                    pe.wait_ge(av_evac, u - 4)
                mm(b[:, 0:256], v0, pt[:, 0:256], start=True, stop=False, skip_group_check=True)
                mm(b[:, 128:256], v1, pt[:, 256:384], start=False, stop=True, skip_group_check=True).then_inc(av_done, 1)
            pe.wait_ge(osq_done, 1)
            for i in range(4):
                ins = mm(ps[:, 4 + i // 2, (i % 2) * 256:(i % 2 + 1) * 256], ones, fm(0, 4)[:, i], start=True, stop=True)
            ins.then_inc(osum_done, 1)
            wait_unit(pe, "pm")
            for i in range(4):
                product_pair(f"ym{i}", unit_view("pm"), 2 * i, 4, qm)
            pe.wait_ge(on_ready, 1)
            wait_unit(pe, "pd")
            for i in range(4):
                product_pair(f"yd{i}", unit_view("pd"), 2 * i, 4, qd)
            for u in range(2):
                wait_unit(pe, f"out{u}")
                pe.wait_ge(merged_ready, 2 * u + 2)
                ins = accumulate(unit_view(f"out{u}"), 4, 4 * u, lambda k: gm[:, k], u == 0, u == 1)
                ins.then_inc(unit_summed, 1)

            norm_sums(6)
            pe.wait_ge(route_in, 32)
            for c in range(TC):
                for k in range(KC):
                    wait_rows(5, k)
                    ins = mm(ps[:, 4, 36 * c:36 * c + 36], hT[:, k, c * P:(c + 1) * P], w_route[:, k], start=(k == 0), stop=(k == KC - 1))
            ins.then_inc(logit_done, 1)
            for q in range(4):
                for j in range(4):
                    ins = nc.tensor.transpose(ps[:, q, j * P:(j + 1) * P], hT[:, 4 * (q % 2) + j, (q // 2) * P:(q // 2 + 1) * P], ident)
                ins.then_inc(htok_pe, 1)
            pe.wait_ge(mask_ready, 1)
            m0, m1 = small[:, 320:352], small[:, 352:384]
            mm(ps[:, 5, 0:32], before, m0, start=True, stop=True)
            mm(ps[:, 5, 32:64], ones, m0, start=True, stop=False)
            mm(ps[:, 5, 32:64], before, m1, start=False, stop=True)
            mm(ps[:, 5, 64:96], ones, m0, start=True, stop=False)
            mm(ps[:, 5, 64:96], ones, m1, start=False, stop=True).then_inc(pos_done, 1)
            pe.wait_ge(htok_ev, 4)
            pe.wait_ge(pick_ready, 1)
            pe.wait_ge(comb_ready, 1)
            for k in range(KC):
                if k >= 4:
                    pe.wait_ge(gather_ev, k - 3)
                for c in range(TC):
                    ins = mm(ps[:, k % 4, :], h2tok[:, c, k * P:(k + 1) * P], pick[:, c], start=(c == 0), stop=(c == TC - 1))
                ins.then_inc(gather_pe, 1)
            for q in range(2):
                for s in range(2):
                    for c in range(TC):
                        ins = nc.tensor.transpose(ps[:, 4 + q, s * 256 + c * P:s * 256 + (c + 1) * P],
                                                  comb[:, c, (2 * q + s) * P:(2 * q + s + 1) * P], ident)
                ins.then_inc(combT_pe, 1)
            pe.wait_ge(gather_ev, KC + 1)
            pe.wait_ge(combT_ev, 2)
            pe.wait_ge(info_ready, 1)

            def pe_window(q, count, e, wg, load):
                pe.wait_ge(xw_ready[q], count + 1)
                for k in range(KC):
                    ins = mm(ps[0:WIN, 0, :], xw[:, k], wg[:, k], start=(k == 0), stop=(k == KC - 1))
                ins.then_inc(gate_done[q], 1)
                loaded = load()

                def up(h):
                    pe.wait_ge(u_lo[h], e + 1)
                    for k in range(KC):
                        for i, (px, pw) in enumerate(PART_PAIRS):
                            ins = mm(ps[0:WIN, 1 + h, 0:256], xp[px][:, k], u_part[pw][:, k, h * 256:(h + 1) * 256],
                                     start=(k == 0 and i == 0), stop=(k == KC - 1 and i == 2))
                    ins.then_inc(up_done[q][h], 1)

                def hidden_transposes(h):
                    pe.wait_ge(hid_done[q][h], count + 1)
                    at = ps[:, 3 * (1 - h)]
                    mm(at[:, 0:WIN], hidE[:, 2 * h * P:(2 * h + 1) * P], ident[0:WIN, 0:WIN], start=True, stop=True)
                    nc.tensor.transpose(at[:, WIN:2 * WIN], hidE[:, (2 * h + 1) * P:(2 * h + 2) * P], ident[0:WIN, 0:WIN]).then_inc(hidT_pe[q][h], 1)

                def down(k, h):
                    for i, (px, pw) in enumerate(PART_PAIRS):
                        ins = mm(ps[0:WIN, 4 + h, :], hidT[px][:, k], d_part[pw][:, k, h * 512:(h + 1) * 512],
                                 start=(k == 0 and i == 0), stop=(k == EC - 1 and i == 2), skip_group_check=True)
                    return ins

                pe.wait_ge(xp_ready[q], count + 1)
                up(0)
                up(1)
                hidden_transposes(0)
                pe.wait_ge(d_lo[0], e + 1)
                pe.wait_ge(y_ev[0][0], e + 1 + q)
                pe.wait_ge(hidT_lo[q][0], count + 1)
                down(0, 0)
                hidden_transposes(1)
                pe.wait_ge(y_ev[0][1], e + 1 + q)
                down(0, 1)
                down(1, 0)
                down(1, 1)
                pe.wait_ge(d_lo[1], e + 1)
                pe.wait_ge(hidT_lo[q][1], count + 1)
                for h in range(2):
                    down(2, h)
                    down(3, h).then_inc(down_done[q][h], 1)
                return loaded

            def expert(e, s, loads):
                pe.wait_ge(g_loaded[s], loads)
                n_more, before_more = pe_window(0, e, e, g_place[s], lambda: more_windows(pe, e))
                with pe.If(n_more > 0), pe.Fori(0, n_more) as w:
                    pe_window(1, before_more + w, e, g_place[s], lambda: None)
                    pe.wait_ge(y_stored[1], 16 * (before_more + w) + 16)

            nc.tensor.nop().then_inc(up_done[0][1], 1)
            with pe.Fori(0, N_EXP // 2) as j:
                for s in range(2):
                    expert(2 * j + s, s, 16 * j + 16)

            pe.wait_ge(ystok_in, 16)
            for f in range(KC):
                for s in range(SC):
                    ins = mm(ps[:, f // 2, (f % 2) * 256:(f % 2 + 1) * 256], ystok[:, s, f * P:(f + 1) * P], combT[:, s], start=(s == 0), stop=(s == SC - 1))
            ins.then_inc(y2_done, 1)
            norm_sums(7)
            for q in range(4):
                for j in range(4):
                    wait_rows(6, 4 * (q % 2) + j)
                    ins = nc.tensor.transpose(ps[:, q, j * P:(j + 1) * P], hT[:, 4 * (q % 2) + j, (q // 2) * P:(q // 2 + 1) * P], ident)
                ins.then_inc(fin_pe, 1)


def constant_arrays():
    i = np.arange(P)
    table = np.zeros((P, N_CONST), np.float32)
    table[:, C_ID:C_ID + P] = np.eye(P)
    table[:, C_AFTER:C_AFTER + P] = i[:, None] > i[None, :]
    table[:, C_BEFORE:C_BEFORE + P] = i[:, None] < i[None, :]
    table[:, C_ONES:C_ONES + P] = 1.0
    half = HD // 2
    for o in range(P):
        if o % HD < half:
            table[o + half, C_ROT + o] = -1.0
        else:
            table[o - half, C_ROT + o] = 1.0
    strict = (i[:, None] < i[None, :]).astype(np.float32)
    table[:, C_STICK:C_STICK + 384] = np.concatenate([strict, np.ones((P, P)), strict], axis=1)
    causal = np.where(i[None, :] <= i[:, None], 0.0, NEG)
    table[:, C_NEG:C_NEG + 384] = np.concatenate([causal, np.zeros((P, P)), causal], axis=1)
    table[:, C_IOTA:] = np.arange(GRP)
    inv = (1.0 / (np.float32(10000.0) ** (np.arange(0, HD, 2, dtype=np.float32) / np.float32(HD)))).astype(np.float32)
    ang = (inv[:, None] * np.arange(SEQ, dtype=np.float32)[None, :]).astype(np.float32)
    ang = ang[i % half]
    rope = np.concatenate([np.cos(ang), np.sin(ang)], axis=1).astype(np.float32)
    slots = np.broadcast_to(np.arange(SLOTS, dtype=np.float32), (P, SLOTS)).copy()
    return {"constants": table, "rope": rope, "slot_numbers": slots}


_INS = ["x", "mix_norm", "ffn_norm", "final_norm", "lru_w_in", "lru_b_in", "lru_conv_w", "lru_conv_b", "lru_gate_w", "lru_gate_b",
        "lru_lambda", "lru_w_out", "lru_b_out", "attn_w_qkv", "attn_w_o", "ffn_w_in", "ffn_w_out", "c_2", "w_ada_2", "b_ada_2",
        "norm1_g_2", "w_in_2", "lambda_q1_2", "lambda_k1_2", "lambda_q2_2", "lambda_k2_2", "diff_subln_g_2", "w_proj_moba_2",
        "w_proj_diff_2", "w_out_2", "norm2_g_2", "w_group_2", "b_group_2", "w_expert_2", "b_expert_2", "w_gate_2", "w_up_2",
        "w_down_2", "final_g_2"]


def kernel(**inputs):
    import concourse.bacc as _bacc
    from concourse.bass_utils import run_bass_kernel_spmd as _run

    nc = _bacc.Bacc("TRN2", target_bir_lowering=False, num_devices=1)
    arrays, aps = {}, {}
    given = {name: np.ascontiguousarray(inputs[name]) for name in _INS}
    for name, array in {**given, **constant_arrays()}.items():
        arrays[f"in_{name}"] = array
        aps[name] = nc.dram_tensor(f"in_{name}", array.shape, mybir.dt.from_np(array.dtype), kind="ExternalInput").ap()
    out = nc.dram_tensor("out", (1, SEQ, D), F32, kind="ExternalOutput").ap()
    ys = nc.dram_tensor("ys", (SLOT_PAD, D), F32).ap()
    program(nc, aps, ys, out)
    result = _run(nc, [arrays], core_ids=[0])
    return result.results[0]["out"]
```
